# Optimizing a Trainium2 kernel written in Bass

```python
import math
import numpy as np
import jax
import jax.numpy as jnp
from jax import lax
import jax, jax.numpy as jnp

D_MODEL = 1024
BATCH = 1
SEQ = 256
DEPTH = 2

HEAD_DIM = 64
MOBA_HEADS = 4
MOBA_BLOCK = 256
MOBA_TOPK = 3
MOBA_QCHUNK = 16
NSA_HEADS = 4
NSA_CMP_LEN = 32
NSA_CMP_STRIDE = 16
NSA_SEL_LEN = 64
NSA_SEL_TOPN = 16
NSA_WINDOW = 512
NSA_QCHUNK = 64
NSA_FORCE_BONUS = 1e4
WIN_QBLOCK = 128
GLA_HEADS = 4
GLA_DK = 64
GLA_DV = 128
GLA_GATE_RANK = 16
GLA_GATE_NORM = 16.0
GLA_CHUNK = 64
N_BRANCH = 3
D_FF = 2816
CONV_WIDTH = 3
REL_BUCKETS = 32
REL_MAX_DIST = 128
N_SOFTMAX_HEADS = MOBA_HEADS + NSA_HEADS

NORM_EPS = 1e-6
NEG_INF = -1e30

SPLIT_SIZES = (
    MOBA_HEADS * HEAD_DIM,
    MOBA_HEADS * HEAD_DIM,
    MOBA_HEADS * HEAD_DIM,
    NSA_HEADS * HEAD_DIM,
    6 * HEAD_DIM,
    NSA_HEADS * 3,
    GLA_HEADS * GLA_DK,
    GLA_HEADS * GLA_DK,
    GLA_HEADS * GLA_DV,
    GLA_GATE_RANK,
    GLA_HEADS * GLA_DV,
    N_BRANCH * D_MODEL,
)
D_IN = sum(SPLIT_SIZES)
SPLIT_POINTS = tuple(int(v) for v in np.cumsum(SPLIT_SIZES)[:-1])


def rms_norm(x, gain):
    xf = x.astype(jnp.float32)
    y = xf * lax.rsqrt(jnp.mean(xf * xf, axis=-1, keepdims=True) + NORM_EPS)
    return (y * gain.astype(jnp.float32)).astype(x.dtype)

def masked_softmax(logits, mask):
    s = jnp.where(mask, logits.astype(jnp.float32), NEG_INF)
    return jax.nn.softmax(s, axis=-1) * mask.astype(jnp.float32)

def rel_bucket(dist):
    n = jnp.maximum(dist, 0)
    max_exact = REL_BUCKETS // 2
    nf = jnp.maximum(n, 1).astype(jnp.float32)
    large = max_exact + (jnp.log(nf / max_exact) / math.log(REL_MAX_DIST / max_exact)
                         * (REL_BUCKETS - max_exact)).astype(jnp.int32)
    large = jnp.minimum(large, REL_BUCKETS - 1)
    return jnp.where(n < max_exact, n, large)

def moba_attention(q, k, v, rel_tab):
    B, S, H, Dh = q.shape
    nb = -(-S // MOBA_BLOCK)
    s_pad = nb * MOBA_BLOCK
    pad = ((0, 0), (0, s_pad - S), (0, 0), (0, 0))
    q, k, v = (jnp.pad(a, pad).transpose(0, 2, 1, 3) for a in (q, k, v))
    kb = k.reshape(B, H, nb, MOBA_BLOCK, Dh)
    vb = v.reshape(B, H, nb, MOBA_BLOCK, Dh)
    k_mean = jnp.mean(kb.astype(jnp.float32), axis=3)
    qblk = jnp.arange(s_pad) // MOBA_BLOCK
    past = jnp.arange(nb)[None, :] < qblk[:, None]
    gate = jnp.where(past, jnp.einsum('bhsd,bhnd->bhsn', q.astype(jnp.float32), k_mean), NEG_INF)
    kk = min(MOBA_TOPK, nb)
    _, sel = lax.top_k(gate, kk)
    sel_valid = jnp.arange(kk)[None, :] < qblk[:, None]
    scale = Dh ** -0.5
    tab_t = rel_tab.T
    head_idx = jnp.arange(H)[None, :, None, None]
    gather_blocks = jax.vmap(jax.vmap(lambda blocks, ix: blocks[ix]))
    n_sel = kk * MOBA_BLOCK

    def chunk(c):
        start = c * MOBA_QCHUNK
        qc = lax.dynamic_slice_in_dim(q, start, MOBA_QCHUNK, axis=2)
        sc = lax.dynamic_slice_in_dim(sel, start, MOBA_QCHUNK, axis=2)
        valid = lax.dynamic_slice_in_dim(sel_valid, start, MOBA_QCHUNK, axis=0)
        tpos = start + jnp.arange(MOBA_QCHUNK)
        own = start // MOBA_BLOCK
        kg = gather_blocks(kb, sc).reshape(B, H, MOBA_QCHUNK, n_sel, Dh)
        vg = gather_blocks(vb, sc).reshape(B, H, MOBA_QCHUNK, n_sel, Dh)
        ko = lax.dynamic_index_in_dim(kb, own, axis=2, keepdims=False)
        vo = lax.dynamic_index_in_dim(vb, own, axis=2, keepdims=False)
        kpos_sel = (sc[..., None] * MOBA_BLOCK + jnp.arange(MOBA_BLOCK)).reshape(B, H, MOBA_QCHUNK, n_sel)
        dist_own = tpos[:, None] - (own * MOBA_BLOCK + jnp.arange(MOBA_BLOCK))[None, :]
        bias_sel = tab_t[head_idx, rel_bucket(tpos[None, None, :, None] - kpos_sel)]
        bias_own = rel_tab[rel_bucket(dist_own)].transpose(2, 0, 1)
        s_sel = jnp.einsum('bhqd,bhqkd->bhqk', qc, kg) * scale + bias_sel
        s_own = jnp.einsum('bhqd,bhkd->bhqk', qc, ko) * scale + bias_own
        mask = jnp.concatenate([jnp.repeat(valid, MOBA_BLOCK, axis=1), dist_own >= 0], axis=-1)
        p = masked_softmax(jnp.concatenate([s_sel, s_own], axis=-1), mask).astype(v.dtype)
        return (jnp.einsum('bhqk,bhqkd->bhqd', p[..., :n_sel], vg)
                + jnp.einsum('bhqk,bhkd->bhqd', p[..., n_sel:], vo))

    out = lax.map(chunk, jnp.arange(s_pad // MOBA_QCHUNK))
    out = out.transpose(1, 2, 0, 3, 4).reshape(B, H, s_pad, Dh).transpose(0, 2, 1, 3)
    return out[:, :S]

def compress_tokens(x, pos_emb, w1, w2):
    B, S, Dh = x.shape
    r = NSA_CMP_LEN // NSA_CMP_STRIDE
    n_cmp = S // NSA_CMP_STRIDE - r + 1
    xs = x.reshape(B, S // NSA_CMP_STRIDE, NSA_CMP_STRIDE, Dh)
    blocks = jnp.concatenate([xs[:, j:j + n_cmp] for j in range(r)], axis=2)
    h = (blocks + pos_emb).reshape(B, n_cmp, NSA_CMP_LEN * Dh)
    return jax.nn.gelu(h @ w1) @ w2

def overlap_matrix(n_cmp, n_blk):
    starts = np.arange(n_cmp) * NSA_CMP_STRIDE
    tok = np.arange(n_blk * NSA_SEL_LEN)
    inside = (tok[None, :] >= starts[:, None]) & (tok[None, :] < starts[:, None] + NSA_CMP_LEN)
    m = inside.reshape(n_cmp, n_blk, NSA_SEL_LEN).sum(-1) / NSA_CMP_LEN
    return jnp.asarray(m, jnp.float32)

def window_attention(q, k, v, rel_tab):
    B, S, H, Dh = q.shape
    nqb = S // WIN_QBLOCK
    nkb = NSA_WINDOW // WIN_QBLOCK
    kp = jnp.pad(k, ((0, 0), (NSA_WINDOW, 0), (0, 0))).reshape(B, nqb + nkb, WIN_QBLOCK, Dh)
    vp = jnp.pad(v, ((0, 0), (NSA_WINDOW, 0), (0, 0))).reshape(B, nqb + nkb, WIN_QBLOCK, Dh)
    kband = jnp.concatenate([kp[:, j:j + nqb] for j in range(nkb + 1)], axis=2)
    vband = jnp.concatenate([vp[:, j:j + nqb] for j in range(nkb + 1)], axis=2)
    qb = q.reshape(B, nqb, WIN_QBLOCK, H, Dh)
    qoff = jnp.arange(WIN_QBLOCK)
    koff = jnp.arange((nkb + 1) * WIN_QBLOCK) - NSA_WINDOW
    dist = qoff[:, None] - koff[None, :]
    kpos = jnp.arange(nqb)[:, None] * WIN_QBLOCK + koff[None, :]
    mask = ((dist >= 0) & (dist < NSA_WINDOW))[None] & (kpos >= 0)[:, None, :]
    bias = rel_tab[rel_bucket(dist)].transpose(2, 0, 1)
    s = jnp.einsum('bnqhd,bnkd->bhnqk', qb, kband) * (Dh ** -0.5) + bias[:, None]
    p = masked_softmax(s, mask).astype(v.dtype)
    return jnp.einsum('bhnqk,bnkd->bnqhd', p, vband).reshape(B, S, H, Dh)

def nsa_attention(q, kc, vc, k_slc, v_slc, k_win, v_win, gates, rel_tab):
    B, S, H, Dh = q.shape
    scale = Dh ** -0.5
    n_cmp = kc.shape[1]
    t = jnp.arange(S)
    cend = jnp.arange(n_cmp) * NSA_CMP_STRIDE + NSA_CMP_LEN - 1
    p_cmp = masked_softmax(jnp.einsum('bshd,bnd->bhsn', q, kc) * scale, cend[None, :] <= t[:, None])
    o_cmp = jnp.einsum('bhsn,bnd->bshd', p_cmp.astype(vc.dtype), vc)
    n_blk = S // NSA_SEL_LEN
    imp = jnp.einsum('bhsn,nj->bsj', p_cmp, overlap_matrix(n_cmp, n_blk))
    cur = t // NSA_SEL_LEN
    blk = jnp.arange(n_blk)[None, :]
    forced = (blk == 0) | (blk == cur[:, None]) | (blk == cur[:, None] - 1)
    imp = jnp.where(blk <= cur[:, None], imp + jnp.where(forced, NSA_FORCE_BONUS, 0.0), NEG_INF)
    n_top = min(NSA_SEL_TOPN, n_blk)
    _, sel = lax.top_k(imp, n_top)
    sel_valid = jnp.arange(n_top)[None, :] < (cur + 1)[:, None]
    ksb = k_slc.reshape(B, n_blk, NSA_SEL_LEN, Dh)
    vsb = v_slc.reshape(B, n_blk, NSA_SEL_LEN, Dh)
    gather_blocks = jax.vmap(lambda blocks, ix: blocks[ix])
    n_keys = n_top * NSA_SEL_LEN

    def chunk(c):
        start = c * NSA_QCHUNK
        qc = lax.dynamic_slice_in_dim(q, start, NSA_QCHUNK, axis=1)
        sc = lax.dynamic_slice_in_dim(sel, start, NSA_QCHUNK, axis=1)
        valid = lax.dynamic_slice_in_dim(sel_valid, start, NSA_QCHUNK, axis=0)
        tpos = start + jnp.arange(NSA_QCHUNK)
        kg = gather_blocks(ksb, sc).reshape(B, NSA_QCHUNK, n_keys, Dh)
        vg = gather_blocks(vsb, sc).reshape(B, NSA_QCHUNK, n_keys, Dh)
        kpos = (sc[..., None] * NSA_SEL_LEN + jnp.arange(NSA_SEL_LEN)).reshape(B, NSA_QCHUNK, n_keys)
        dist = tpos[None, :, None] - kpos
        bias = rel_tab[rel_bucket(dist)].transpose(0, 3, 1, 2)
        mask = (dist >= 0) & jnp.repeat(valid, NSA_SEL_LEN, axis=1)[None]
        s = jnp.einsum('bqhd,bqkd->bhqk', qc, kg) * scale + bias
        p = masked_softmax(s, mask[:, None]).astype(vg.dtype)
        return jnp.einsum('bhqk,bqkd->bqhd', p, vg)

    o_slc = lax.map(chunk, jnp.arange(S // NSA_QCHUNK))
    o_slc = o_slc.transpose(1, 0, 2, 3, 4).reshape(B, S, H, Dh)
    o_win = window_attention(q, k_win, v_win, rel_tab)
    return gates[..., 0:1] * o_cmp + gates[..., 1:2] * o_slc + gates[..., 2:3] * o_win

def gla_attention(q, k, v, log_a):
    B, S, H, Dk = q.shape
    Dv = v.shape[-1]
    n_chunk = S // GLA_CHUNK

    def to_chunks(a):
        return a.astype(jnp.float32).reshape(B, n_chunk, GLA_CHUNK, H, -1).transpose(1, 0, 3, 2, 4)

    qc, kc, vc, gc = (to_chunks(a) for a in (q * (Dk ** -0.5), k, v, log_a))
    causal = jnp.tril(jnp.ones((GLA_CHUNK, GLA_CHUNK), dtype=bool))

    def step(state, inp):
        qi, ki, vi, gi = inp
        b = jnp.cumsum(gi, axis=2)
        decay = jnp.exp(jnp.where(causal[:, :, None], b[:, :, :, None, :] - b[:, :, None, :, :], NEG_INF))
        a_intra = jnp.einsum('bhid,bhjd,bhijd->bhij', qi, ki, decay)
        o = (jnp.einsum('bhij,bhjv->bhiv', a_intra, vi)
             + jnp.einsum('bhid,bhdv->bhiv', qi * jnp.exp(b), state))
        b_last = b[:, :, -1:, :]
        new_state = (state * jnp.exp(b_last[:, :, 0, :, None])
                     + jnp.einsum('bhjd,bhjv->bhdv', ki * jnp.exp(b_last - b), vi))
        return new_state, o

    state0 = jnp.zeros((B, H, Dk, Dv), jnp.float32)
    _, o = lax.scan(step, state0, (qc, kc, vc, gc))
    return o.transpose(1, 0, 3, 2, 4).reshape(B, S, H, Dv)

def hybrid_mixer(h, rel_bias, w_in, moba_q_norm, moba_k_norm, nsa_q_norm, nsa_k_norm,
                 cmp_pos_k, cmp_pos_v, cmp_k_w1, cmp_k_w2, cmp_v_w1, cmp_v_w2,
                 gla_gate_w, gla_gate_b, gla_out_norm,
                 w_branch_moba, w_branch_nsa, w_branch_gla, w_out):
    B, S, _ = h.shape
    (mq, mk, mv, nq, nkv, ngate, gq, gk, gv, g_lr, g_out, merge) = jnp.split(h @ w_in, SPLIT_POINTS, axis=-1)

    def heads(a, n):
        return a.reshape(B, S, n, -1)

    o_moba = moba_attention(rms_norm(heads(mq, MOBA_HEADS), moba_q_norm),
                            rms_norm(heads(mk, MOBA_HEADS), moba_k_norm),
                            heads(mv, MOBA_HEADS), rel_bias[:, :MOBA_HEADS]).reshape(B, S, -1)
    k_c, v_c, k_s, v_s, k_w, v_w = jnp.split(nkv, 6, axis=-1)
    kc = rms_norm(compress_tokens(k_c, cmp_pos_k, cmp_k_w1, cmp_k_w2), nsa_k_norm[0])
    vc = compress_tokens(v_c, cmp_pos_v, cmp_v_w1, cmp_v_w2)
    o_nsa = nsa_attention(rms_norm(heads(nq, NSA_HEADS), nsa_q_norm), kc, vc,
                          rms_norm(k_s, nsa_k_norm[1]), v_s, rms_norm(k_w, nsa_k_norm[2]), v_w,
                          jax.nn.sigmoid(heads(ngate, NSA_HEADS)), rel_bias[:, MOBA_HEADS:]).reshape(B, S, -1)
    log_a = jax.nn.log_sigmoid((g_lr @ gla_gate_w + gla_gate_b).astype(jnp.float32)) / GLA_GATE_NORM
    o_gla = gla_attention(heads(gq, GLA_HEADS), heads(gk, GLA_HEADS), heads(gv, GLA_HEADS),
                          heads(log_a, GLA_HEADS)).astype(h.dtype)
    o_gla = (rms_norm(o_gla, gla_out_norm) * jax.nn.silu(heads(g_out, GLA_HEADS))).reshape(B, S, -1)
    g_a, g_b, g_c = jnp.split(jax.nn.sigmoid(merge), N_BRANCH, axis=-1)
    z = g_a * (o_moba @ w_branch_moba) + g_b * (o_nsa @ w_branch_nsa) + g_c * (o_gla @ w_branch_gla)
    return z @ w_out

def conv_ffn(h, w_up, conv_w, conv_b, w_down):
    a, g = jnp.split(h @ w_up, 2, axis=-1)
    a = lax.conv_general_dilated(a, conv_w[:, None, :].astype(a.dtype), (1,), [(CONV_WIDTH - 1, 0)],
                                 dimension_numbers=('NWC', 'WIO', 'NWC'), feature_group_count=D_FF) + conv_b
    return (jax.nn.gelu(a) * g) @ w_down

def first_inputs(seed: int = 0) -> dict:
    key = jax.random.key(seed)
    ks = jax.random.split(key, 32)
    L = DEPTH
    qkv_w = MOBA_HEADS * HEAD_DIM

    def nrm(k, shape, scale):
        return jax.random.normal(k, shape, jnp.float32) * scale

    def gain(k, shape):
        return 1.0 + 0.02 * jax.random.normal(k, shape, jnp.float32)

    return {
        "x": nrm(ks[0], (BATCH, SEQ, D_MODEL), 1.0),
        "rel_bias": nrm(ks[1], (REL_BUCKETS, N_SOFTMAX_HEADS), 0.1),
        "attn_norm": gain(ks[2], (L, D_MODEL)),
        "w_in": nrm(ks[3], (L, D_MODEL, D_IN), D_MODEL ** -0.5),
        "moba_q_norm": gain(ks[4], (L, HEAD_DIM)),
        "moba_k_norm": gain(ks[5], (L, HEAD_DIM)),
        "nsa_q_norm": gain(ks[6], (L, HEAD_DIM)),
        "nsa_k_norm": gain(ks[7], (L, 3, HEAD_DIM)),
        "cmp_pos_k": nrm(ks[8], (L, NSA_CMP_LEN, HEAD_DIM), 0.1),
        "cmp_pos_v": nrm(ks[9], (L, NSA_CMP_LEN, HEAD_DIM), 0.1),
        "cmp_k_w1": nrm(ks[10], (L, NSA_CMP_LEN * HEAD_DIM, HEAD_DIM), (NSA_CMP_LEN * HEAD_DIM) ** -0.5),
        "cmp_k_w2": nrm(ks[11], (L, HEAD_DIM, HEAD_DIM), HEAD_DIM ** -0.5),
        "cmp_v_w1": nrm(ks[12], (L, NSA_CMP_LEN * HEAD_DIM, HEAD_DIM), (NSA_CMP_LEN * HEAD_DIM) ** -0.5),
        "cmp_v_w2": nrm(ks[13], (L, HEAD_DIM, HEAD_DIM), HEAD_DIM ** -0.5),
        "gla_gate_w": nrm(ks[14], (L, GLA_GATE_RANK, GLA_HEADS * GLA_DK), GLA_GATE_RANK ** -0.5),
        "gla_gate_b": nrm(ks[15], (L, GLA_HEADS * GLA_DK), 0.1),
        "gla_out_norm": gain(ks[16], (L, GLA_DV)),
        "w_branch_moba": nrm(ks[17], (L, qkv_w, D_MODEL), qkv_w ** -0.5),
        "w_branch_nsa": nrm(ks[18], (L, NSA_HEADS * HEAD_DIM, D_MODEL), (NSA_HEADS * HEAD_DIM) ** -0.5),
        "w_branch_gla": nrm(ks[19], (L, GLA_HEADS * GLA_DV, D_MODEL), (GLA_HEADS * GLA_DV) ** -0.5),
        "w_out": nrm(ks[20], (L, D_MODEL, D_MODEL), D_MODEL ** -0.5),
        "ffn_norm": gain(ks[21], (L, D_MODEL)),
        "w_up": nrm(ks[22], (L, D_MODEL, 2 * D_FF), D_MODEL ** -0.5),
        "conv_w": nrm(ks[23], (L, CONV_WIDTH, D_FF), CONV_WIDTH ** -0.5),
        "conv_b": nrm(ks[24], (L, D_FF), 0.02),
        "w_down": nrm(ks[25], (L, D_FF, D_MODEL), D_FF ** -0.5),
    }

def first_block(x, rel_bias, attn_norm, w_in, moba_q_norm, moba_k_norm, nsa_q_norm, nsa_k_norm,
              cmp_pos_k, cmp_pos_v, cmp_k_w1, cmp_k_w2, cmp_v_w1, cmp_v_w2,
              gla_gate_w, gla_gate_b, gla_out_norm,
              w_branch_moba, w_branch_nsa, w_branch_gla, w_out,
              ffn_norm, w_up, conv_w, conv_b, w_down):
    for l in range(DEPTH):
        h = rms_norm(x, attn_norm[l])
        x = x + hybrid_mixer(h, rel_bias, w_in[l], moba_q_norm[l], moba_k_norm[l], nsa_q_norm[l], nsa_k_norm[l],
                             cmp_pos_k[l], cmp_pos_v[l], cmp_k_w1[l], cmp_k_w2[l], cmp_v_w1[l], cmp_v_w2[l],
                             gla_gate_w[l], gla_gate_b[l], gla_out_norm[l],
                             w_branch_moba[l], w_branch_nsa[l], w_branch_gla[l], w_out[l])
        h = rms_norm(x, ffn_norm[l])
        x = x + conv_ffn(h, w_up[l], conv_w[l], conv_b[l], w_down[l])
    return x


CHUNK = 64
N_MIXERS = 2
D_FF_2 = 256 * ((8 * D_MODEL // 3 + 255) // 256)
RMS_EPS = 1e-6
L2_EPS = 1e-6
SC_WIDTH = 3
GDN_HEAD_DIM = 128
GDN_K_HEADS = D_MODEL // 128
GDN_V_HEADS = 2 * GDN_K_HEADS
GDN_KEY_DIM = GDN_K_HEADS * GDN_HEAD_DIM
GDN_VAL_DIM = GDN_V_HEADS * GDN_HEAD_DIM
GDN_CONV_WIDTH = 4
GDN_CONV_DIM = 2 * GDN_KEY_DIM + GDN_VAL_DIM
GDN_IN_DIM = GDN_CONV_DIM + GDN_VAL_DIM + 2 * GDN_V_HEADS
N_SC_LAYERS = (DEPTH + 1) // 2
N_GDN_LAYERS = DEPTH // 2
N_NORMS = 6


def rms_norm_2(x, g):
    xf = x.astype(jnp.float32)
    y = xf * lax.rsqrt(jnp.mean(xf * xf, axis=-1, keepdims=True) + RMS_EPS)
    return (y * g.astype(jnp.float32)).astype(x.dtype)

def causal_depthwise_conv(x, w):
    k, c = w.shape
    return lax.conv_general_dilated(
        x, w[:, None, :].astype(x.dtype), window_strides=(1,), padding=[(k - 1, 0)],
        dimension_numbers=("NWC", "WIO", "NWC"), feature_group_count=c)

def swiglu(x, w_gate_up, w_down):
    gate, up = jnp.split(x @ w_gate_up, 2, axis=-1)
    return (jax.nn.silu(gate) * up) @ w_down

def short_conv_mixer(x, w_in, conv_w, w_out):
    b, c, v = jnp.split(x @ w_in, 3, axis=-1)
    y = b * causal_depthwise_conv(c * v, conv_w)
    return y @ w_out

def l2norm(x):
    return x * lax.rsqrt(jnp.sum(x * x, axis=-1, keepdims=True) + L2_EPS)

def chunk_gated_delta_rule(q, k, v, g, beta):
    bsz, nh, t, dk = q.shape
    dv = v.shape[-1]
    n = t // CHUNK
    q = q * (dk ** -0.5)

    def rs(a):
        return a.reshape(bsz, nh, n, CHUNK, *a.shape[3:])

    q, k, v, g, beta = rs(q), rs(k), rs(v), rs(g), rs(beta)
    g = jnp.cumsum(g, axis=-1)
    k_beta = k * beta[..., None]
    v_beta = v * beta[..., None]
    idx = jnp.arange(CHUNK)
    causal = idx[:, None] >= idx[None, :]
    strict = idx[:, None] > idx[None, :]
    decay = jnp.exp(jnp.where(causal, g[..., :, None] - g[..., None, :], -jnp.inf))
    a = jnp.where(strict, jnp.einsum("bhncd,bhnsd->bhncs", k_beta, k) * decay, 0.0)
    eye = jnp.eye(CHUNK, dtype=q.dtype)
    t_inv = lax.linalg.triangular_solve(eye + a, jnp.broadcast_to(eye, a.shape),
                                        left_side=True, lower=True)
    u = jnp.einsum("bhncs,bhnse->bhnce", t_inv, v_beta)
    w = jnp.einsum("bhncs,bhnsd->bhncd", t_inv, k_beta * jnp.exp(g)[..., None])
    qk = jnp.where(causal, jnp.einsum("bhncd,bhnsd->bhncs", q, k) * decay, 0.0)
    q_g = q * jnp.exp(g)[..., None]
    g_last = g[..., -1]
    k_tail = k * jnp.exp(g_last[..., None] - g)[..., None]

    def step(state, inp):
        q_g_n, qk_n, u_n, w_n, k_tail_n, gl_n = inp
        v_new = u_n - jnp.einsum("bhcd,bhde->bhce", w_n, state)
        o = jnp.einsum("bhcd,bhde->bhce", q_g_n, state) + jnp.einsum("bhcs,bhse->bhce", qk_n, v_new)
        state = state * jnp.exp(gl_n)[..., None, None] + jnp.einsum("bhcd,bhce->bhde", k_tail_n, v_new)
        return state, o

    xs = tuple(jnp.moveaxis(a_, 2, 0) for a_ in (q_g, qk, u, w, k_tail, g_last))
    s0 = jnp.zeros((bsz, nh, dk, dv), dtype=q.dtype)
    _, o = lax.scan(step, s0, xs)
    return jnp.moveaxis(o, 0, 2).reshape(bsz, nh, t, dv)

def gated_deltanet_mixer(x, w_in, conv_w, a_log, dt_bias, norm_w, w_out):
    bsz, t, _ = x.shape
    proj = x @ w_in
    qkv, z, b, a = jnp.split(proj, [GDN_CONV_DIM, GDN_CONV_DIM + GDN_VAL_DIM,
                                    GDN_CONV_DIM + GDN_VAL_DIM + GDN_V_HEADS], axis=-1)
    qkv = jax.nn.silu(causal_depthwise_conv(qkv, conv_w))
    q, k, v = jnp.split(qkv.astype(jnp.float32), [GDN_KEY_DIM, 2 * GDN_KEY_DIM], axis=-1)
    rep = GDN_V_HEADS // GDN_K_HEADS
    q = jnp.repeat(l2norm(q.reshape(bsz, t, GDN_K_HEADS, GDN_HEAD_DIM)), rep, axis=2)
    k = jnp.repeat(l2norm(k.reshape(bsz, t, GDN_K_HEADS, GDN_HEAD_DIM)), rep, axis=2)
    v = v.reshape(bsz, t, GDN_V_HEADS, GDN_HEAD_DIM)
    beta = jax.nn.sigmoid(b.astype(jnp.float32))
    g = -jnp.exp(a_log.astype(jnp.float32)) * jax.nn.softplus(
        a.astype(jnp.float32) + dt_bias.astype(jnp.float32))
    o = chunk_gated_delta_rule(q.transpose(0, 2, 1, 3), k.transpose(0, 2, 1, 3),
                               v.transpose(0, 2, 1, 3), g.transpose(0, 2, 1),
                               beta.transpose(0, 2, 1))
    o = o.transpose(0, 2, 1, 3)
    o = o * lax.rsqrt(jnp.mean(o * o, axis=-1, keepdims=True) + RMS_EPS) * norm_w.astype(jnp.float32)
    o = o * jax.nn.silu(z.astype(jnp.float32).reshape(bsz, t, GDN_V_HEADS, GDN_HEAD_DIM))
    return o.reshape(bsz, t, GDN_VAL_DIM).astype(x.dtype) @ w_out

def second_inputs(seed: int = 0) -> dict:
    key = jax.random.key(seed)
    ks = jax.random.split(key, 16)
    f32 = jnp.float32
    d = D_MODEL
    x = jax.random.normal(ks[0], (BATCH, SEQ, d), f32)
    norm_g = 1.0 + 0.02 * jax.random.normal(ks[1], (DEPTH, N_NORMS, d), f32)
    ffn_w_gate_up = jax.random.normal(ks[2], (DEPTH, 2, d, 2 * D_FF_2), f32) * d ** -0.5
    ffn_w_down = jax.random.normal(ks[3], (DEPTH, 2, D_FF_2, d), f32) * D_FF_2 ** -0.5
    sc_w_in = jax.random.normal(ks[4], (N_SC_LAYERS, d, 3 * d), f32) * d ** -0.5
    sc_conv_w = jax.random.normal(ks[5], (N_SC_LAYERS, SC_WIDTH, d), f32) * SC_WIDTH ** -0.5
    sc_w_out = jax.random.normal(ks[6], (N_SC_LAYERS, d, d), f32) * d ** -0.5
    gdn_w_in = jax.random.normal(ks[7], (N_GDN_LAYERS, d, GDN_IN_DIM), f32) * d ** -0.5
    gdn_conv_w = jax.random.normal(ks[8], (N_GDN_LAYERS, GDN_CONV_WIDTH, GDN_CONV_DIM), f32) * GDN_CONV_WIDTH ** -0.5
    gdn_a_log = jnp.log(jax.random.uniform(ks[9], (N_GDN_LAYERS, GDN_V_HEADS), f32, 1.0, 16.0))
    gdn_dt_bias = 1.0 + 0.1 * jax.random.normal(ks[10], (N_GDN_LAYERS, GDN_V_HEADS), f32)
    gdn_norm_w = 1.0 + 0.02 * jax.random.normal(ks[11], (N_GDN_LAYERS, GDN_HEAD_DIM), f32)
    gdn_w_out = jax.random.normal(ks[12], (N_GDN_LAYERS, GDN_VAL_DIM, d), f32) * GDN_VAL_DIM ** -0.5
    return {"x": x, "norm_g": norm_g, "ffn_w_gate_up": ffn_w_gate_up, "ffn_w_down": ffn_w_down,
            "sc_w_in": sc_w_in, "sc_conv_w": sc_conv_w, "sc_w_out": sc_w_out,
            "gdn_w_in": gdn_w_in, "gdn_conv_w": gdn_conv_w, "gdn_a_log": gdn_a_log,
            "gdn_dt_bias": gdn_dt_bias, "gdn_norm_w": gdn_norm_w, "gdn_w_out": gdn_w_out}

def second_block(x, norm_g, ffn_w_gate_up, ffn_w_down, sc_w_in, sc_conv_w, sc_w_out,
              gdn_w_in, gdn_conv_w, gdn_a_log, gdn_dt_bias, gdn_norm_w, gdn_w_out):
    h = x
    for i in range(DEPTH):
        g = norm_g[i]
        ff = swiglu(rms_norm_2(h, g[0]), ffn_w_gate_up[i, 0], ffn_w_down[i, 0])
        h = h + 0.5 * rms_norm_2(ff, g[1])
        m_in = rms_norm_2(h, g[2])
        j = i // N_MIXERS
        if i % N_MIXERS == 0:
            mix = short_conv_mixer(m_in, sc_w_in[j], sc_conv_w[j], sc_w_out[j])
        else:
            mix = gated_deltanet_mixer(m_in, gdn_w_in[j], gdn_conv_w[j], gdn_a_log[j],
                                       gdn_dt_bias[j], gdn_norm_w[j], gdn_w_out[j])
        h = h + rms_norm_2(mix, g[3])
        ff = swiglu(rms_norm_2(h, g[4]), ffn_w_gate_up[i, 1], ffn_w_down[i, 1])
        h = h + 0.5 * rms_norm_2(ff, g[5])
    return h


def setup_inputs(seed=0):
    out = dict(first_inputs(seed))
    for name, value in second_inputs(seed + 1).items():
        if name != "x":
            out[name + "_2"] = value
    return out


def reference(
    x, rel_bias, attn_norm, w_in, moba_q_norm, moba_k_norm, nsa_q_norm, nsa_k_norm, cmp_pos_k,
    cmp_pos_v, cmp_k_w1, cmp_k_w2, cmp_v_w1, cmp_v_w2, gla_gate_w, gla_gate_b, gla_out_norm,
    w_branch_moba, w_branch_nsa, w_branch_gla, w_out, ffn_norm, w_up, conv_w, conv_b, w_down,
    norm_g_2, ffn_w_gate_up_2, ffn_w_down_2, sc_w_in_2, sc_conv_w_2, sc_w_out_2, gdn_w_in_2,
    gdn_conv_w_2, gdn_a_log_2, gdn_dt_bias_2, gdn_norm_w_2, gdn_w_out_2,
):
    x = first_block(
        x, rel_bias, attn_norm, w_in, moba_q_norm, moba_k_norm, nsa_q_norm, nsa_k_norm,
        cmp_pos_k, cmp_pos_v, cmp_k_w1, cmp_k_w2, cmp_v_w1, cmp_v_w2, gla_gate_w, gla_gate_b,
        gla_out_norm, w_branch_moba, w_branch_nsa, w_branch_gla, w_out, ffn_norm, w_up, conv_w,
        conv_b, w_down,
    )
    return second_block(
        x, norm_g_2, ffn_w_gate_up_2, ffn_w_down_2, sc_w_in_2, sc_conv_w_2, sc_w_out_2,
        gdn_w_in_2, gdn_conv_w_2, gdn_a_log_2, gdn_dt_bias_2, gdn_norm_w_2, gdn_w_out_2,
    )


_drawn_inputs = setup_inputs


def setup_inputs(seed=0):
    import zlib

    import numpy as np

    out = dict(_drawn_inputs(seed))
    spreads = {}
    factors = {'moba_q_norm': 8.0,
     'moba_k_norm': 8.0,
     'nsa_q_norm': 8.0,
     'nsa_k_norm': 8.0,
     'cmp_pos_k': 5.227,
     'gla_out_norm': 3.057,
     'gdn_dt_bias_2': 64.0,
     'gdn_norm_w_2': 40.046,
     'gdn_a_log_2': 8.0}
    for name, (base, spread) in spreads.items():
        noise = np.random.default_rng([zlib.crc32(name.encode()), seed]).standard_normal(out[name].shape)
        drawn = base * np.exp(spread * noise) if base else spread * noise
        out[name] = jnp.asarray(drawn.astype(out[name].dtype))
    for name, factor in factors.items():
        out[name] = (out[name] * factor).astype(out[name].dtype)
    return out
```

```python
import concourse.bass as bass
from concourse import mybir
from contextlib import ExitStack

P = 128
D = 1024
S = 256
KT = D // P
DEPTH = 2
FF = 2816
FT = FF // P
RING = 6
EPS = 1e-6

F32 = mybir.dt.float32
F32R = mybir.dt.float32r
U8 = mybir.dt.uint8
ALU = mybir.AluOpType
ACT = mybir.ActivationFunctionType
AX = mybir.AxisListType

FFN1, FFN2, SHORT, DELTA, HYBRID = "ffn1", "ffn2", "short_conv", "delta", "hybrid"


def stage_list():
    out = []
    for layer in range(DEPTH):
        out += [(HYBRID, layer), (FFN1, layer)]
    for layer in range(DEPTH):
        out += [(FFN2, 2 * layer), ((SHORT, DELTA)[layer % 2], 0), (FFN2, 2 * layer + 1)]
    return out


KH = 8
VH = 2 * KH
KSET = 2
SET = 2 * KSET
SETS = KH // KSET
CHUNKS = S // P
ROW_A = 32
WIDTH = 4
LEVELS = (2, 4, 8, 16, 32, 64)
NEG = -1e30
ARENA = 18944

HEADS = 4
HD = 64
CMP = 32
STEP = 16
NCMP = S // STEP - CMP // STEP + 1
RANK = 16
GATE_NORM = 16.0
ROW_G = 32
BUCKETS = 32
TABLE = 3 * P
SEGMENTS = (256, 128, 64, 32, 16, 8, 4, 2, 0)

QK_TILES = (2, 3, 4, 5, 7, 8, 9, 10)
TOKEN_TILES = (6, 11, 12, 17, 18, 19, 20)
VALUE_PAIRS = (11, 17, 19)
FIRST_GLA, FIRST_OUT_GATE, FIRST_MERGE = 13, 21, 25
TILES = FIRST_MERGE + 3 * KT
SLOTS = TILES - FIRST_GLA
ATTN_SLOT, LEVEL_SLOT, OUT_SLOT = 7, 20, 29

KC_STEPS = ("kc_copied", "kc_squared", "kc_sum", "kc_ms", "kc_root", "kc_ready")
CMP_STEPS = ("cmp_scores", "cmp_max", "cmp_exp", "cmp_p", "cmp_turned", "cmp_pt", "cmp_pt2", "cmp_o")
GATE_STEPS = ("gate_product", "gate_in", "gate_exp", "gate_ln")
GLA_STEPS = ("gla_sums", "gla_ms", "gla_root", "gla_inv")

PANELS = {FFN1: 3 * FT, FFN2: 3 * FT, SHORT: 4 * KT, DELTA: 1 + 8 * SETS + 2 * VH, HYBRID: TILES + 2 * KT}
BLOCKS = {FFN1: FT, FFN2: FT, SHORT: KT, DELTA: VH, HYBRID: KT}


def column_map(stages):
    at, n = {}, 0

    def add(key, count):
        nonlocal n
        at[key] = n
        n += count
    for s, (kind, i) in enumerate(stages):
        add(("pre", s), KT)
        if kind in (FFN2, SHORT, DELTA):
            add(("post", s), KT)
        if kind == HYBRID:
            add(("qk_gain", s), 8)
            add(("cmp_gain", s), 1)
            add(("gate_b", s), 2)
            add(("gla_gain", s), 1)
        if kind == FFN1:
            add(("tap", s), 3 * FT)
            add(("conv_b", s), FT)
        if kind == SHORT:
            add(("tap", s), 3 * KT)
        if kind == DELTA:
            add(("tap", s), WIDTH * 4 * KH)
            add(("out_norm", s), 1)
            add(("a_log", s), 1)
            add(("dt_bias", s), 1)
    return at, n


def delta_tiles(n):
    return [KSET * n + j for j in range(KSET)] + [KH + KSET * n + j for j in range(KSET)] + \
        [2 * KH + SET * n + j for j in range(SET)]


def constants():
    import numpy as np
    i, j = np.arange(P)[:, None], np.arange(P)[None, :]
    out = [i == j]
    for s in LEVELS:
        out.append((i // (2 * s) == j // (2 * s)) & (i // s % 2 == 1) & (j // s % 2 == 0))
    out.append((i // 2 == j // 2) & (j % 2 == 1) & (i % 2 == 0))
    out.append(np.where(j > i, 0.0, NEG))
    return np.stack([m.astype(np.float32) for m in out], 1)


def hybrid_constants():
    import math
    import numpy as np
    j, i = np.arange(P)[:, None], np.arange(P)[None, :]
    level = [(i // g == j // g) & (j % g < g // 2) & (i % g >= g // 2) for g in SEGMENTS[1:-1]] + [i == j]
    dist = np.arange(S - 1, S - 1 - TABLE, -1)
    n = np.maximum(dist, 0)
    exact = BUCKETS // 2
    f = np.float32
    large = exact + (np.log(np.maximum(n, 1).astype(f) / f(exact)) / f(math.log(128 / exact))
                     * f(BUCKETS - exact)).astype(np.int32)
    bucket = np.where(n < exact, n, np.minimum(large, BUCKETS - 1))
    onehot = -((bucket[None, :] == np.arange(BUCKETS)[:, None]) & (dist >= 0)).astype(f)
    masked = np.broadcast_to(np.where(dist < 0, -NEG, 0.0).astype(f), (2 * HEADS, TABLE))
    token = np.arange(S).reshape(CHUNKS, P).T[:, :, None]
    seen = np.arange(NCMP + 1)[None, None, :] * STEP + CMP - 1 <= token
    seen = seen[:, :, 0:NCMP]
    cmp_masks = np.stack([seen.astype(f), np.where(seen, 0.0, -NEG).astype(f)], 1)
    halves = (np.arange(P)[:, None] // HD == np.arange(2)[None, :]).astype(f)
    return {
        "level_masks_in": np.stack(level, 1).astype(np.float32),
        "onehot_in": onehot, "masked_in": np.ascontiguousarray(masked),
        "cmp_masks_in": np.ascontiguousarray(np.broadcast_to(cmp_masks[:, :, None], (P, 2, 4, CHUNKS, NCMP))),
        "halves_in": halves,
    }


def hybrid_inputs(w):
    import numpy as np

    def diagonal(k, v):
        out = np.zeros(k.shape[:1] + (P, CMP, P), k.dtype)
        out[:, 0:HD, :, 0:HD] = k.reshape(-1, CMP, HD, HD).transpose(0, 2, 1, 3)
        out[:, HD:, :, HD:] = v.reshape(-1, CMP, HD, HD).transpose(0, 2, 1, 3)
        return out
    return {
        **hybrid_constants(),
        "rel_in": w["rel_bias"],
        "w1_in": diagonal(w["cmp_k_w1"], w["cmp_v_w1"]),
        "w2_in": np.concatenate([np.concatenate([w[n], w[n]], 2) for n in ("cmp_k_w2", "cmp_v_w2")], 1),
        "pos_in": np.concatenate([w["cmp_pos_k"].transpose(0, 2, 1), w["cmp_pos_v"].transpose(0, 2, 1)], 1),
        "gate_w_in": w["gla_gate_w"],
    }


def lay_out(stages, w):
    import numpy as np

    def ups(m, t):
        return m[:, t * P:(t + 1) * P].reshape(KT, P, P).transpose(1, 0, 2).reshape(P, KT * P)

    def downs(m, t):
        return m[t * P:(t + 1) * P, :]

    def columns(v):
        return v.reshape(-1, P).T

    panels, cols = [], []
    for kind, i in stages:
        if kind == HYBRID:
            w_in = w["w_in"][i]
            at = dict(mq=0, mk=256, mv=512, nq=768, nkv=1024, ngate=1408, gq=1420, gk=1676, gv=1932, glr=2444,
                      gout=2460, merge=2972)

            def take(*spans):
                return ups(np.concatenate([w_in[:, a:a + n] for a, n in spans], 1), 0)
            low = np.zeros((D, P), w_in.dtype)
            low[:, 0:RANK] = w_in[:, at["glr"]:at["glr"] + RANK]
            low[:, ROW_G:ROW_G + 3 * HEADS] = w_in[:, at["ngate"]:at["ngate"] + 3 * HEADS]
            kc, vc, ks, vs, kw, vw = (at["nkv"] + HD * j for j in range(6))
            panels += [ups(low, 0), take((kc, 2 * HD)), take((ks, HD), (ks, HD)), take((kw, HD), (kw, HD)),
                       take((at["nq"], P)), take((at["nq"] + P, P)), take((vs, HD), (vw, HD))]
            for name, n in (("mq", 2), ("mk", 2), ("mv", 2), ("gq", 2), ("gk", 2), ("gv", 4), ("gout", 4),
                            ("merge", 24)):
                if name in ("mv", "gv"):
                    for j in range(0, n, 2):
                        both = w_in[:, at[name] + P * j:at[name] + P * (j + 2)]
                        both = both.reshape(2, KT // 2, P, 2 * P).transpose(0, 2, 1, 3).reshape(2, P, KT * P)
                        panels += [both[0], both[1]]
                else:
                    panels += [take((at[name] + P * j, P)) for j in range(n)]
            branch = np.concatenate([w["w_branch_moba"][i], w["w_branch_nsa"][i], w["w_branch_gla"][i]], 0)
            for f in range(KT):
                panels.append(ups(branch, f))
                if f:
                    panels.append(downs(w["w_out"][i], f - 1))
            panels.append(downs(w["w_out"][i], KT - 1))
            twice = lambda v: np.concatenate([v, v])[:, None]
            nk = w["nsa_k_norm"][i]
            cols += [columns(w["attn_norm"][i])]
            cols += [twice(v) for v in (nk[1], nk[2], w["nsa_q_norm"][i], w["nsa_q_norm"][i], w["moba_q_norm"][i],
                                        w["moba_q_norm"][i], w["moba_k_norm"][i], w["moba_k_norm"][i], nk[0])]
            cols += [columns(w["gla_gate_b"][i]), columns(w["gla_out_norm"][i])]
        if kind == FFN1:
            cols.append(columns(w["ffn_norm"][i]))
            up, down, tiles = w["w_up"][i], w["w_down"][i], (0, FT)
        if kind == FFN2:
            at = 4 * (i % 2)
            cols += [columns(w["norm_g_2"][i // 2, at + j]) for j in range(2)]
            up, down, tiles = w["ffn_w_gate_up_2"][i // 2, i % 2], w["ffn_w_down_2"][i // 2, i % 2], (0, FT)
        if kind in (SHORT, DELTA):
            cols += [columns(w["norm_g_2"][int(kind == DELTA), 2 + j]) for j in range(2)]
        if kind == SHORT:
            up, down, tiles = w["sc_w_in_2"][0], w["sc_w_out_2"][0], (KT, 2 * KT, 0)
        if kind in (FFN1, FFN2, SHORT):
            nb = KT if kind == SHORT else FT
            for f in range(nb):
                panels += [ups(up, t + f) for t in tiles]
                if f:
                    panels.append(downs(down, f - 1))
            panels.append(downs(down, nb - 1))
        if kind == DELTA:
            w_in, w_out = w["gdn_w_in_2"][0], w["gdn_w_out_2"][0]
            gates = np.zeros((D, P), w_in.dtype)
            gates[:, 0:VH] = w_in[:, 6 * D:6 * D + VH]
            gates[:, ROW_A:ROW_A + VH] = w_in[:, 6 * D + VH:]
            panels.append(ups(gates, 0))
            order = [t for n in range(SETS) for t in delta_tiles(n)]
            panels += [ups(w_in, t) for t in order]
            for f in range(VH):
                panels.append(ups(w_in, 4 * KH + f))
                if f:
                    panels.append(downs(w_out, f - 1))
            panels.append(downs(w_out, VH - 1))
            conv_cols = w["gdn_conv_w_2"][0].reshape(WIDTH, 4 * KH, P)[:, order].reshape(-1, P).T
            late = np.zeros((P, 2), w_in.dtype)
            late[ROW_A:ROW_A + VH, 0] = w["gdn_a_log_2"][0]
            late[ROW_A:ROW_A + VH, 1] = w["gdn_dt_bias_2"][0]
            cols += [conv_cols, columns(w["gdn_norm_w_2"][0]), late]
        if kind == FFN1:
            cols += [columns(w["conv_w"][i]), columns(w["conv_b"][i])]
        if kind == SHORT:
            cols.append(columns(w["sc_conv_w_2"][0]))
    return {
        "x_in": np.ascontiguousarray(w["x"][0].T.reshape(KT, P, S).transpose(1, 0, 2)),
        "panels": np.stack(panels),
        "masks_in": constants(),
        **hybrid_inputs(w),
        "cols_in": np.ascontiguousarray(np.concatenate(cols, 1)),
    }


def build(nc, stages, arrays):
    x_in, panels, cols_in, out = (arrays[n] for n in ("x_in", "panels", "cols_in", "out"))
    masks_in = arrays["masks_in"]
    n_panels = panels.shape[0]
    n_stages = len(stages)
    col_at, n_cols = column_map(stages)
    first_panel, first_block = [], []
    p = b = 0
    for kind, _ in stages:
        first_panel.append(p)
        first_block.append(b)
        p += PANELS[kind]
        b += BLOCKS[kind]
    assert p == n_panels

    with ExitStack() as ctx:
        def sb(name, shape, dt=F32):
            return ctx.enter_context(nc.sbuf_tensor(name, shape, dt))

        def sem(name):
            return ctx.enter_context(nc.semaphore(name))

        bank = [ctx.enter_context(nc.psum_tensor(f"bank{i}", [P, 512], F32)) for i in range(8)]

        def acc(m):
            return bank[m // 2][:, (m % 2) * S:(m % 2) * S + S]

        raw = [sb(f"raw{i}", [P, KT * P]) for i in range(RING)]
        whi = [sb(f"whi{i}", [P, KT * P], F32R) for i in range(RING)]
        wlo = [sb(f"wlo{i}", [P, KT * P], F32R) for i in range(RING)]
        cols = sb("cols", [P, n_cols])
        ones = sb("ones", [P, P])
        x = sb("x", [P, KT, S])
        xhi = sb("xhi", [P, KT, S], F32R)
        xlo = sb("xlo", [P, KT, S], F32R)
        sq = sb("sq", [P, 4, S])
        psq = sb("psq", [P, 2, 512])
        ms = sb("ms", [P, S])
        rt = sb("rt", [P, S])
        rstd = sb("rstd", [P, S])
        prstd = sb("prstd", [P, S])
        root_of_one = sb("root_of_one", [P, n_stages])
        tmp = sb("tmp", [P, 2, S])
        first = sb("first", [P, 2, S + 2])
        second = sb("second", [P, 2, S])
        third = sb("third", [P, 2, S])
        conv = sb("conv", [P, 2, S])
        act_out = sb("act_out", [P, 2, S])
        h = sb("h", [P, 2, S])
        hhi = sb("hhi", [P, 2, S], F32R)
        hlo = sb("hlo", [P, 2, S], F32R)

        masks = sb("masks", [P, len(LEVELS) + 3, P])
        ident = masks[:, 0, :]
        arena = sb("arena", [P, ARENA])
        carved = [0]

        def carve(name, shape):
            size = 1
            for w in shape[1:]:
                size *= w
            assert carved[0] + size <= ARENA, (name, carved[0] + size)
            view = arena[0:shape[0], carved[0]:carved[0] + size]
            carved[0] += size
            if len(shape) == 2:
                return view
            names = "abc"[:len(shape) - 1]
            return view.rearrange("p (" + " ".join(names) + ") -> p " + " ".join(names),
                                  **{n: w for n, w in zip(names, shape[1:])})

        delta_in = carve("delta_in", [P, 2, S + WIDTH - 1])
        qk = [carve(f"qk{i}", [P, 2 * KSET, S]) for i in range(2)]
        qk_sq = sq
        v_feat = carve("v_feat", [P, SET, S])
        v_tok = [carve(f"v_tok{c}", [P, SET, P]) for c in range(CHUNKS)]
        gates = carve("gates", [ROW_A + VH, 4, S])
        a_rate = carve("a_rate", [ROW_A + VH, 1])
        g_tok = carve("g_tok", [P, CHUNKS, VH])
        beta_tok = carve("beta_tok", [P, CHUNKS, VH])
        neg_beta = carve("neg_beta", [P, CHUNKS, VH])
        neg_eg = carve("neg_eg", [P, CHUNKS, VH])
        norm_cols = carve("norm_cols", [P, 2, 2 * KSET * CHUNKS])
        inv_norm = carve("inv_norm", [P, 2 * KSET * CHUNKS])
        decay = carve("decay", [P, SET, CHUNKS, P])
        eg_row = carve("eg_row", [P, SET, P])
        amat = carve("amat", [P, SET, CHUNKS, P])
        qmat = carve("qmat", [P, SET, CHUNKS, P])
        tri = carve("tri", [P, SET, CHUNKS, P])
        tri_t = carve("tri_t", [P, SET, CHUNKS, P])
        wmat = carve("wmat", [P, SET, CHUNKS, P])
        k_tok = carve("k_tok", [P, KSET, P])
        k_tail = carve("k_tail", [P, SET, P])
        v_new = [carve(f"v_new{c}", [P, SET, P]) for c in range(CHUNKS)]
        state = carve("state", [P, SET, P])
        o_all = carve("o_all", [P, VH, S])
        o_norm = carve("o_norm", [P, 2, VH * CHUNKS])
        o_inv = carve("o_inv", [P, VH * CHUNKS])


        carved[0] = 0
        rel = carve("rel", [P, 2 * HEADS, S])
        qkn = carve("qkn", [P, 8, S])
        mv = carve("mv", [P, CHUNKS, S])
        vsw = carve("vsw", [P, CHUNKS, P])
        gv = carve("gv", [P, CHUNKS, HEADS * P])
        gqk = carve("gqk", [P, 4, S])
        gsum = carve("gsum", [P, 2, S])
        a_diag = [carve(f"a_diag{b}", [P, 4, P]) for b in range(2)]
        a_cross = carve("a_cross", [P, 2, 2, P])
        sgate = carve("sgate", [P, HEADS, S])
        merge = carve("merge", [P, 3 * KT, S])
        o_moba = carve("o_moba", [P, 2, S])
        o_slc = carve("o_slc", [P, 2, S])
        o_win = carve("o_win", [P, 2, S])
        o_cmp = carve("o_cmp", [P, 2, S])
        lowrank = carve("lowrank", [ROW_G + 3 * HEADS, S])
        level_masks = carve("level_masks", [P, 8 * P // 4]).bitcast(U8).rearrange("p (a b) -> p a b", a=8)
        cmp_masks = carve("cmp_masks", [P, 2, 2 * 2 * CHUNKS * NCMP])
        w1 = merge[:, 8:24, :].rearrange("p a b -> p (a b)").rearrange("p (c d) -> p c d", c=CMP)
        cmp_x = sgate[:, 0:2, :].rearrange("p a b -> p (a b)").rearrange("p (c d) -> p c d", c=CMP)
        mask_words = merge[:, 4:8, :].rearrange("p a b -> p (a b)").rearrange("p (a b) -> p a b", a=8)
        onehot = merge[0:BUCKETS, 0:2, :].rearrange("p a b -> p (a b)")[:, 0:TABLE]
        table = merge[0:2 * HEADS, 2:4, :].rearrange("p a b -> p (a b)")[:, 0:TABLE]
        gate_w = o_moba[0:RANK, 0, :]
        pos = o_moba[:, 1, 0:CMP]
        w2 = o_moba[:, 1, CMP:CMP + P]
        flat2 = lambda t: t[:, :, :].rearrange("p a b -> p (a b)")
        logits = psq
        probs = [flat2(second), flat2(third)]
        probs_t = [flat2(conv), flat2(act_out)]
        cmp_t = [h[0:NCMP, :, :].rearrange("p a b -> p (a b)"), tmp[0:NCMP, :, :].rearrange("p a b -> p (a b)")]
        ones_row = ones[:, 0:1].to_broadcast([P, S])
        level_q = [third[:, :, :], psq[:, 0, :].rearrange("p (a b) -> p a b", a=2)]
        level_k = [conv[:, :, :], psq[:, 1, :].rearrange("p (a b) -> p a b", a=2)]
        kcv = tmp[:, 0, :]
        cmp_small = act_out[:, :, :].rearrange("p a b -> p (a b)")
        cmp_hid = cmp_small[:, 16:16 + NCMP]
        cmp_raw, cmp_k = cmp_small[:, 64:64 + NCMP], cmp_small[:, 80:80 + NCMP]
        cmp_sq, cmp_ms = cmp_small[:, 96:96 + NCMP], cmp_small[:, 112:112 + NCMP]
        cmp_v = cmp_small[0:NCMP, 128:128 + HD]
        cmp_p = cmp_small[:, 192:192 + 8 * NCMP].rearrange("p (a b) -> p a b", a=8)
        cmp_max, cmp_sum = cmp_small[:, 320:328], cmp_small[:, 328:336]
        o_gla = gqk

        def mixed(k):
            return o_moba[:, k, :] if k < 2 else o_cmp[:, k - 2, :] if k < 4 else o_gla[:, k - 4, :]

        rel_table = sb("rel_table", [BUCKETS, 2 * HEADS])
        halves = sb("halves", [P, 2])
        rstd_tok = sb("rstd_tok", [P, CHUNKS])
        qk_gain = sb("qk_gain", [P, 8])
        gla_gain = sb("gla_gain", [P, 1])
        qk_ms = sb("qk_ms", [P, 2, 32])
        qk_inv = sb("qk_inv", [P, 32])
        row_min = sb("row_min", [P, 2, 2])
        row_sum = sb("row_sum", [P, 2, 2])
        row_inv = sb("row_inv", [P, 2, 2])
        scratch = nc.dram_tensor("bias_table", [2 * HEADS, P, TABLE + 1], F32, kind="Internal").ap()

        y = {name: sem("y_" + name) for name in (
            "consts table_product table stored rel_loaded small_loaded tile_read tok_read tok_rstd turned "
            "gla_gained squared qk_sums qk_ms qk_root qk_inv qk_rows qk_ready gains low_tanh gsum cmp_x "
            "cmp_hidden cmp_bias cmp_act cmp_kv vc_copied o_cmp s_sum t_ready p_ready p_scaled gated "
            "nsa_gated p_turned pt_ready o_sum o_copied zeroed diff e_abs e_ready qe_ready level_sum a_ready "
            "out_th sgate merged gate_rows nsa gla_sum gla_copied gla_squared gla_rows gla_ready o_hi o_lo "
            "kc_norm cmp_attn low_gate gla_norm".split())}
        masks_loaded = sem("masks_loaded")
        d = {name: sem("d_" + name) for name in (
            "tile_read tap convolved activated squared gates_scaled gate_act gate_seq gates_ready gate_turned "
            "gate_tok tok_exp norm_sums norm_ms norm_root norm_inv norm_rows qk_ready v_turned v_copied "
            "g_rows exponent decay eg products amat tri0 tri0_turned tri_ready decay_diag qmat k_turned k_copied "
            "k_tail w_sum w_ready t_sum u_sum t_ready u_ready r0 v0 s1 s1_copied ks v1_in r1 v1 qg o_sum o_copied "
            "o_squared o_sums o_added o_root o_inv o_rows").split()}
        x_loaded = sem("x_loaded")
        cols_loaded = sem("cols_loaded")
        landed = [sem(f"landed{i}") for i in range(RING)]
        hi_done = sem("hi_done")
        lo_done = sem("lo_done")
        panel_used = sem("panel_used")
        acc_ready = sem("acc_ready")
        consts_ready = sem("consts_ready")
        x_updated = sem("x_updated")
        sq_ready = sem("sq_ready")
        xhi_ready = sem("xhi_ready")
        xlo_ready = sem("xlo_ready")
        sum_ready = sem("sum_ready")
        ms_ready = sem("ms_ready")
        root_ready = sem("root_ready")
        rstd_ready = sem("rstd_ready")
        psq_ready = sem("psq_ready")
        psq_used = sem("psq_used")
        post_ms_ready = sem("post_ms_ready")
        post_root_ready = sem("post_root_ready")
        dve_seq = sem("dve_seq")
        gate_scaled = sem("gate_scaled")
        pair_read = sem("pair_read")
        product_done = sem("product_done")
        tap_done = sem("tap_done")
        conv_done = sem("conv_done")
        conv_seq = sem("conv_seq")
        act_done = sem("act_done")
        h_done = sem("h_done")
        hhi_done = sem("hhi_done")
        hlo_done = sem("hlo_done")
        stored = sem("stored")

        def col(key, i=0):
            c = col_at[key] + i
            return cols[:, c:c + 1]

        UNROLL = 2

        def plus(n, turn, step):
            return n if turn is None else turn * step + n

        def n_up(s):
            return {SHORT: 3, DELTA: 1, HYBRID: 1}.get(stages[s][0], 2)

        def n_blocks(s):
            return BLOCKS[stages[s][0]]

        def before_blocks(s):
            return PANELS[stages[s][0]] - n_blocks(s) * (n_up(s) + 1)

        def up_panel(s, f, j):
            return first_panel[s] + before_blocks(s) + (f * (n_up(s) + 1) - 1 if f else 0) + j

        def down_panel(s, f):
            return up_panel(s, f + 1, n_up(s)) if f + 1 < n_blocks(s) \
                else first_panel[s] + PANELS[stages[s][0]] - 1

        def used(p, turn=None):
            return plus(p + 1, turn, RING)

        def loops(s):
            return stages[s][0] in (FFN1, FFN2)

        def lead(s):
            return 3 if post_norm(s) else 2

        def post_norm(s):
            return stages[s][0] in (FFN2, SHORT, DELTA)

        def posts_before(s):
            return sum(post_norm(t) for t in range(s))

        def convs_before(s):
            return sum(n_blocks(t) for t in range(s) if stages[t][0] in (FFN1, SHORT))

        def acts_before(s):
            return sum(n_blocks(t) for t in range(s) if stages[t][0] in (FFN1, FFN2, DELTA))

        def products_before(s):
            return sum(n_blocks(t) for t in range(s) if stages[t][0] == SHORT)

        def run_blocks(eng, s, body):
            nb = n_blocks(s)
            if not loops(s):
                for f in range(nb):
                    body(f, None)
                return
            body(0, None)
            body(1, None)
            with eng.Fori(0, (nb - 4) // UNROLL) as turn:
                for f in range(2, 2 + UNROLL):
                    body(f, turn)
            body(nb - 2, None)
            body(nb - 1, None)

        def wait_x(eng, s, k):
            if s == 0:
                eng.wait_ge(x_loaded, 16)
            else:
                eng.wait_ge(x_updated, KT * (s - 1) + k + 1)

        def wait_acc(eng, s, q):
            if q < KT // 2 - 1:
                eng.wait_ge(acc_ready, 3 * s + q + 1)
            else:
                eng.wait_ge(panel_used, used(first_panel[s] + PANELS[stages[s][0]] - 1))

        def hybrids_before(s):
            return sum(stages[t][0] == HYBRID for t in range(s))

        def tok_tiles(t):
            return sum(u < t for u in TOKEN_TILES)

        def unit(t):
            return t - sum(u < t for u in VALUE_PAIRS)

        def tok_units(t):
            return sum(u < t and u not in VALUE_PAIRS for u in TOKEN_TILES)

        N_TOK = len(TOKEN_TILES) - len(VALUE_PAIRS)

        def feature_tile(t):
            if t == 0:
                return lowrank
            if t == 1:
                return kcv
            if t in QK_TILES:
                return qkn[:, QK_TILES.index(t), :]
            if t < TOKEN_TILES[3]:
                return gqk[:, t - FIRST_GLA, :]
            if t < FIRST_MERGE:
                return sgate[:, t - FIRST_OUT_GATE, :]
            return merge[:, t - FIRST_MERGE, :]

        def attn(u):
            kind, a, b = u // HEADS, u % HEADS // 2, u % 2
            head = 2 * a + b
            if kind < 2:
                return 2 + a, kind, b, HEADS + head, vsw[:, :, kind * HD:(kind + 1) * HD], (o_slc, o_win)[kind][:, a, :]
            return 4 + a, 6 + a, b, head, mv[:, :, head * HD:(head + 1) * HD], o_moba[:, a, :]

        def half(b):
            return slice(HD * b, HD * b + HD)

        def chunk(c):
            return slice(c * P, (c + 1) * P)

        NU = 3 * HEADS
        NL = len(SEGMENTS)

        def tap(s, t, f, turn):
            c = col_at[("tap", s)] + t * n_blocks(s) + f
            return cols[:, c:c + 1] if turn is None else cols[:, bass.ds(turn * UNROLL + c, 1)]

        def conv_bias(s, f, turn):
            c = col_at[("conv_b", s)] + f
            return cols[:, c:c + 1] if turn is None else cols[:, bass.ds(turn * UNROLL + c, 1)]

        block = ctx.enter_context(nc.Block())

        @block.sync
        def _(sp):
            sp.dma_start(x[:], x_in).then_inc(x_loaded, 16)
            sp.dma_start(cols[:], cols_in).then_inc(cols_loaded, 16)
            sp.dma_start(masks[:], masks_in).then_inc(masks_loaded, 16)
            for j in range(RING):
                sp.dma_start(raw[j][:], panels[j]).then_inc(landed[j], 16)
            turns = n_panels // RING - 1
            with sp.Fori(0, turns) as i:
                for j in range(RING):
                    sp.wait_ge(lo_done, i * RING + (j + 1))
                    sp.dma_start(raw[j][:], panels[bass.ds(i * RING + (RING + j), 1), :, :].rearrange(
                        "a p n -> (a p) n")).then_inc(landed[j], 16)
            for p in range((turns + 1) * RING, n_panels):
                sp.wait_ge(lo_done, p - RING + 1)
                sp.dma_start(raw[p % RING][:], panels[p]).then_inc(landed[p % RING], 16)
            sp.wait_ge(x_updated, KT * n_stages)
            sp.dma_start(out, x[:]).then_inc(stored, 16)
            sp.wait_ge(stored, 16)

        @block.gpsimd
        def _(pool):
            pool.memset(ones[:], 1.0).then_inc(consts_ready, 1)
            pool.memset(first[:, :, 0:2], 0.0).then_inc(consts_ready, 1)
            pool.wait_ge(masks_loaded, 16)
            one = masks[:, 0:1, :].to_broadcast([P, 2 * CHUNKS, P])

            def hybrid(s):
                n = hybrids_before(s)
                v = lambda name, i, per: pool.wait_ge(y[name], per * n + i + 1)
                layer = stages[s][1]
                if n == 0:
                    for dst, name in ((rel_table[:], "rel_in"), (onehot, "onehot_in"), (table, "masked_in"),
                                      (mask_words, "level_masks_in"),
                                      (cmp_masks, "cmp_masks_in"),
                                      (halves[:], "halves_in")):
                        src = arrays[name]
                        if name == "cmp_masks_in":
                            src = src.rearrange("p a b c n -> p a (b c n)")
                        pool.dma_start(dst, src).then_inc(y["consts"], 16)
                else:
                    pool.wait_ge(h_done, first_block[s - 2] + KT)
                for dst, name in ((w1, "w1_in"), (w2, "w2_in"), (pos, "pos_in"), (gate_w, "gate_w_in")):
                    pool.dma_start(dst, arrays[name][layer]).then_inc(y["small_loaded"], 16)
                if n == 0:
                    for b in range(2):
                        pool.memset(a_diag[b], 0.0).then_inc(y["zeroed"], 1)
                    pool.wait_ge(y["consts"], 16 * 6)
                    pool.tensor_copy(level_masks, mask_words).then_inc(y["zeroed"], 1)
                    pool.wait_ge(y["table"], 1)
                    pool.dma_start(scratch[:, :, 0:TABLE], table.rearrange("h (a n) -> h a n", a=1)
                                   .to_broadcast([2 * HEADS, P, TABLE])).then_inc(y["stored"], 16)
                    pool.wait_ge(y["stored"], 16)
                    pool.dma_start(rel, bass.AP(scratch.tensor, P - 1, [[TABLE, P], [P * (TABLE + 1), 2 * HEADS],
                                                                       [1, S]])) \
                        .then_inc(y["rel_loaded"], 16)
                for li in range(NL - 1):
                    v("e_ready", li, NL - 1)
                    if li >= 2:
                        v("level_sum", li - 2, NL)
                    elif li == 0:
                        v("o_sum", NU - 1, NU)
                    decay_ = first[:, :, 2:]
                    pool.tensor_tensor(level_q[li % 2], gqk[:, 0:2, :], decay_, ALU.mult).then_inc(y["qe_ready"], 1)
                    if li == 0:
                        pool.tensor_tensor(level_k[0], gqk[:, 2:4, :], decay_, ALU.mult).then_inc(y["qe_ready"], 1)

            for s in range(n_stages):
                if stages[s][0] == HYBRID:
                    hybrid(s)
                if stages[s][0] != DELTA:
                    continue
                if hybrids_before(s):
                    pool.wait_ge(x_updated, KT * (1 + max(t for t in range(s) if stages[t][0] == HYBRID)))
                pool.memset(delta_in[:, :, 0:WIDTH - 1], 0.0).then_inc(consts_ready, 1)
                for n in range(SETS):
                    v = lambda name, i, per: pool.wait_ge(d[name], per * n + i + 1)
                    for g in range(KSET):
                        flat = decay[:, 2 * g:2 * g + 2, :, :].rearrange("p h c n -> p (h c) n")
                        v("amat", g, 2)
                        pool.tensor_tensor(flat, flat, one, ALU.add).then_inc(d["decay_diag"], 1)
                    v("decay_diag", 1, 2)
                    v("qmat", 1, 4)
                    for g in range(KSET):
                        for hh in range(2):
                            last = pool.tensor_tensor(qmat[:, 2 * g + hh, :, :],
                                                      tmp[:, g, :].rearrange("p (c i) -> p c i", c=2),
                                                      decay[:, 2 * g + hh, :, :], ALU.mult)
                        last.then_inc(d["qmat"], 1)
                    v("eg", 1, 2)
                    v("qk_ready", 1, 2)
                    for g in range(KSET):
                        for hh in range(2):
                            last = pool.tensor_tensor(eg_row[:, 2 * g + hh, :], eg_row[:, 2 * g + hh, :],
                                                      qk[n % 2][:, g, P:], ALU.mult)
                    last.then_inc(d["qg"], 1)

        @block.scalar
        def _(act):
            split = [0]

            def hi(p, turn=None):
                slot = p % RING
                act.wait_ge(landed[slot], plus(16 * (p // RING + 1), turn, 16))
                if p >= RING:
                    act.wait_ge(panel_used, used(p - RING, turn))
                act.activation(whi[slot][:], raw[slot][:], ACT.Copy).then_inc(hi_done, 1)

            def hi_to(last):
                for p in range(split[0], min(last + 1, n_panels)):
                    hi(p)
                split[0] = max(split[0], last + 1)

            def prepare(s):
                for k in range(KT):
                    n = s * KT + k
                    wait_x(act, s, k)
                    if n >= 4:
                        act.wait_ge(sum_ready, n - 3)
                    act.activation(sq[:, n % 4, :], x[:, k, :], ACT.Square).then_inc(sq_ready, 1)
                    act.activation(xhi[:, k, :], x[:, k, :], ACT.Copy, scale=col(("pre", s), k)) \
                        .then_inc(xhi_ready, 1)
                act.wait_ge(ms_ready, s + 1)
                act.activation(rt[:], ms[:], ACT.Sqrt).then_inc(root_ready, 1)

            def finish(s):
                act.activation(root_of_one[:, s:s + 1], ones[:, 0:1], ACT.Sqrt)
                if not post_norm(s):
                    return
                n = posts_before(s)
                for q in range(KT // 2):
                    wait_acc(act, s, q)
                    if 4 * n + q >= 2:
                        act.wait_ge(psq_used, 4 * n + q - 1)
                    act.activation(psq[:, q % 2, :], bank[q][:], ACT.Square).then_inc(psq_ready, 1)
                act.wait_ge(post_ms_ready, n + 1)
                act.activation(rt[:], ms[:], ACT.Sqrt).then_inc(post_root_ready, 1)

            def ffn_block(s, f, turn):
                kind, sl = stages[s][0], f % 2
                b = plus(first_block[s] + f, turn, UNROLL)
                if kind != HYBRID:
                    act.wait_ge(gate_scaled, b + 1)
                if kind in (FFN2, DELTA):
                    act.activation(act_out[:, sl, :], first[:, sl, 2:], ACT.Silu).then_inc(act_done, 1)
                elif kind != HYBRID:
                    c = plus(convs_before(s) + f, turn, UNROLL)
                    if kind == FFN1:
                        act.activation(conv[:, sl, :], first[:, sl, 2:], ACT.Identity,
                                       scale=tap(s, 2, f, turn), bias=conv_bias(s, f, turn)) \
                            .then_inc(tap_done, 1)
                        act.wait_ge(conv_done, c + 1)
                        act.activation(act_out[:, sl, :], conv[:, sl, :], ACT.Gelu_apprx_tanh) \
                            .then_inc(act_done, 1)
                    else:
                        act.activation(conv[:, sl, :], first[:, sl, 2:], ACT.Copy,
                                       scale=tap(s, 2, f, turn)).then_inc(tap_done, 1)
                act.wait_ge(h_done, b + 1)
                if f >= 2:
                    act.wait_ge(panel_used, used(down_panel(s, f - 2), turn))
                act.activation(hhi[:, sl, :], h[:, sl, :], ACT.Copy).then_inc(hhi_done, 1)

            def blocks_of(s):
                def body(f, turn):
                    nb = n_blocks(s)
                    if turn is not None:
                        for j in range(n_up(s) + 1):
                            hi(up_panel(s, f + 1, j), turn)
                        split[0] = up_panel(s, nb - 2, n_up(s)) + 1
                    elif f + 1 < nb:
                        hi_to(up_panel(s, f + 1, n_up(s)))
                    else:
                        hi_to(down_panel(s, f))
                    ffn_block(s, f, turn)
                    if f == nb - 1:
                        hi_to(down_panel(s, f) + lead(s))
                run_blocks(act, s, body)

            def hybrid(s):
                n = hybrids_before(s)
                v = lambda name, i, per: act.wait_ge(y[name], per * n + i + 1)
                p0 = first_panel[s]
                n_feat = TILES - len(TOKEN_TILES)

                def tile(t):
                    if t in TOKEN_TILES:
                        if t in VALUE_PAIRS:
                            return
                        i = tok_units(t)
                        act.wait_ge(panel_used, used(p0 + t))
                        if i == 0:
                            v("tok_rstd", 0, 1)
                        src = bank[4 + unit(t) % 2]
                        for c in range(CHUNKS):
                            w = P if i == 0 else S
                            dst = (vsw, mv, gv[:, :, 0:S], gv[:, :, S:])[i][:, c, :]
                            last = act.activation(dst, src[:, c * w:(c + 1) * w], ACT.Copy,
                                                  scale=rstd_tok[:, c:c + 1])
                        last.then_inc(y["tok_read"], 1)
                        return
                    v("tile_read", t - tok_tiles(t), n_feat)
                    if t in QK_TILES:
                        i = QK_TILES.index(t)
                        if i >= 4:
                            v("qk_sums", 0, 2)
                        act.activation(sq[:, i % 4, :], qkn[:, i, :], ACT.Square).then_inc(y["squared"], 1)
                    elif t >= FIRST_MERGE:
                        g = merge[:, t - FIRST_MERGE, :]
                        act.activation(g, g, ACT.Tanh, scale=0.5).then_inc(y["merged"], 1)
                    elif t >= FIRST_OUT_GATE:
                        i = t - FIRST_OUT_GATE
                        act.activation(sq[:, i, :], sgate[:, i, :], ACT.Tanh, scale=0.5).then_inc(y["out_th"], 1)

                def step(k):
                    u = k - ATTN_SLOT
                    if k == 0:
                        g = lowrank[ROW_G:ROW_G + 3 * HEADS, :]
                        act.activation(g, g, ACT.Tanh, scale=0.5).then_inc(y["low_tanh"], 1)
                        v("low_gate", GATE_STEPS.index("gate_in"), len(GATE_STEPS))
                        act.activation(conv[:, :, :], conv[:, :, :], ACT.Exp, scale=-1.0).then_inc(y["low_gate"], 1)
                        v("low_gate", GATE_STEPS.index("gate_exp"), len(GATE_STEPS))
                        act.activation(conv[:, :, :], conv[:, :, :], ACT.Ln, bias=1.0).then_inc(y["low_gate"], 1)
                        v("qk_ms", 0, 1)
                        act.activation(qk_ms[:, 1, :], qk_ms[:, 0, :], ACT.Sqrt).then_inc(y["qk_root"], 1)
                        v("cmp_bias", 0, 1)
                        act.activation(cmp_hid, bank[0][:, 0:NCMP], ACT.Gelu_apprx_tanh,
                                       bias=cmp_small[:, 0:1]).then_inc(y["cmp_act"], 1)
                    if k == 2:
                        v("kc_norm", KC_STEPS.index("kc_copied"), len(KC_STEPS))
                        act.activation(cmp_sq, cmp_raw, ACT.Square).then_inc(y["kc_norm"], 1)
                    if k == 3:
                        v("kc_norm", KC_STEPS.index("kc_ms"), len(KC_STEPS))
                        act.activation(cmp_ms, cmp_ms, ACT.Sqrt).then_inc(y["kc_norm"], 1)
                    if k == 4:
                        v("cmp_attn", CMP_STEPS.index("cmp_max"), len(CMP_STEPS))
                        act.activation(cmp_p, cmp_p, ACT.Exp, scale=-1.0).then_inc(y["cmp_attn"], 1)
                    if k == 6:
                        v("cmp_attn", CMP_STEPS.index("cmp_turned"), len(CMP_STEPS))
                        for b in range(2):
                            act.activation(cmp_t[b], bank[2 + b][0:NCMP, :], ACT.Copy).then_inc(y["cmp_attn"], 1)
                    if k == 7:
                        v("cmp_attn", CMP_STEPS.index("cmp_o"), len(CMP_STEPS))
                        act.activation(o_cmp, bank[6][:].rearrange("p (a t) -> p a t", a=2), ACT.Copy) \
                            .then_inc(y["o_cmp"], 1)
                    if 0 <= u < NU:
                        b = u % 2
                        v("t_ready", u, NU)
                        if u >= 2:
                            v("p_turned", u - 2, NU)
                        for r, cs in enumerate((slice(0, P), slice(P, 3 * P))):
                            last = act.activation(probs[b][:, cs], logits[:, b, cs], ACT.Exp, scale=-1.0,
                                                  bias=row_min[:, b, r:r + 1], accum_out=row_sum[:, b, r:r + 1])
                        last.then_inc(y["p_ready"], 1)
                    if 0 <= u - 1 < NU:
                        w = u - 1
                        v("p_turned", w, NU)
                        if w >= 2:
                            v("o_sum", w - 2, NU)
                        act.activation(probs_t[w % 2][:, 0:3 * P], bank[2 + w % 2][:, 0:3 * P], ACT.Copy) \
                            .then_inc(y["pt_ready"], 1)
                    if 0 <= u - 2 < NU and u % 2:
                        w = u - 2
                        v("o_sum", w, NU)
                        act.activation(attn(w)[5], bank[6 + w // 2 % 2][:, 0:S], ACT.Copy).then_inc(y["o_copied"], 1)
                    li = k - LEVEL_SLOT + 1
                    if 0 <= li < NL - 1:
                        v("diff", li, NL - 1)
                        dif = second[:, :, :]
                        act.activation(dif, dif, ACT.Abs).then_inc(y["e_abs"], 1)
                        v("e_abs", li, NL - 1)
                        if li:
                            act.wait_ge(y["qe_ready"], 2 * ((NL - 1) * n + li))
                        act.activation(first[:, :, 2:], dif, ACT.Exp, scale=-1.0 / GATE_NORM).then_inc(y["e_ready"], 1)
                    if k == OUT_SLOT:
                        for g in range(2):
                            v("gla_sum", g, 2)
                            og = o_gla[:, 2 * g:2 * g + 2, :]
                            act.activation(og, bank[6 + g][:].rearrange("p (a t) -> p a t", a=2), ACT.Copy) \
                                .then_inc(y["gla_copied"], 1)
                            v("gla_copied", g, 2)
                            act.activation(sq[:, 2 * g:2 * g + 2, :], og, ACT.Square).then_inc(y["gla_squared"], 1)
                    if k == OUT_SLOT + 1:
                        v("gla_norm", GLA_STEPS.index("gla_ms"), len(GLA_STEPS))
                        act.activation(qk_ms[:, 1, 0:8], qk_ms[:, 0, 0:8], ACT.Sqrt).then_inc(y["gla_norm"], 1)

                for t in range(TILES):
                    hi_to(p0 + t + 3)
                    if t >= FIRST_GLA:
                        step(t - FIRST_GLA)
                    tile(t)
                act.wait_ge(panel_used, used(p0 + TILES - 1))
                v("nsa", 0, 1)
                v("gla_ready", 1, 2)
                for k in range(KT):
                    act.activation(xhi[:, k, :], mixed(k), ACT.Copy).then_inc(y["o_hi"], 1)
                hi_to(p0 + TILES + 3)

            def delta_tile(s, n, j):
                t, sl = 8 * n + j, j % 2
                act.wait_ge(d["tile_read"], t + 1)
                act.activation(conv[:, sl, :], delta_in[:, sl, WIDTH - 1:], ACT.Copy,
                               scale=col(("tap", s), (WIDTH - 1) * 4 * KH + t)).then_inc(d["tap"], 1)
                act.wait_ge(d["convolved"], t + 1)
                if j < 2 * KSET:
                    act.activation(qk[n % 2][:, j, :], conv[:, sl, :], ACT.Silu).then_inc(d["activated"], 1)
                    act.wait_ge(d["activated"], t + 1)
                    act.activation(qk_sq[:, j, :], qk[n % 2][:, j, :], ACT.Square).then_inc(d["squared"], 1)
                else:
                    act.activation(v_feat[:, j - 2 * KSET, :], conv[:, sl, :], ACT.Silu).then_inc(d["activated"], 1)

            def delta_slot(s, n, j):
                p = first_panel[s] + 1 + 8 * (n + 1) + j
                hi_to(min(p + 3, first_panel[s] + before_blocks(s) + 4))
                if n + 1 < SETS:
                    delta_tile(s, n + 1, j)

            def delta_gates(s):
                a, b = slice(ROW_A, ROW_A + VH), slice(0, VH)
                act.wait_ge(d["gates_scaled"], 2)
                act.activation(gates[b, 1, :], gates[b, 0, :], ACT.Exp, scale=-1.0).then_inc(d["gate_act"], 1)
                act.activation(gates[a, 2, :], gates[a, 1, :], ACT.Exp, scale=-1.0).then_inc(d["gate_act"], 1)
                act.activation(a_rate[a, :], col(("a_log", s))[a, :], ACT.Exp).then_inc(d["gate_act"], 1)
                act.wait_ge(d["gate_act"], 2)
                act.activation(gates[a, 3, :], gates[a, 2, :], ACT.Ln, bias=1.0).then_inc(d["gate_act"], 1)

            def delta_norm_root(n):
                act.wait_ge(d["norm_ms"], 2 * (n + 1))
                act.activation(norm_cols[:, 1, :], norm_cols[:, 0, :], ACT.Sqrt).then_inc(d["norm_root"], 1)

            def delta_set(s, n):
                v = lambda name, i, per: act.wait_ge(d[name], per * n + i + 1)
                for c in range(CHUNKS):
                    v("v_turned", c, 2)
                    act.activation(v_tok[c][:], bank[c][:].rearrange("p (h e) -> p h e", h=SET), ACT.Copy) \
                        .then_inc(d["v_copied"], 1)
                delta_slot(s, n, 0)
                for g in range(KSET):
                    v("exponent", g, 2)
                    act.activation(eg_row[:, 2 * g:2 * g + 2, :],
                                   bank[6 + g][:].rearrange("p (h c i) -> p h c i", h=2, c=2)[:, :, 1, :],
                                   ACT.Exp).then_inc(d["eg"], 1)
                for g in range(KSET):
                    v("exponent", g, 2)
                    act.activation(decay[:, 2 * g:2 * g + 2, :, :], decay[:, 2 * g:2 * g + 2, :, :], ACT.Exp) \
                        .then_inc(d["decay"], 1)
                delta_slot(s, n, 1)
                for g in range(KSET):
                    v("amat", g, 2)
                    act.activation(tmp[:, g, :], bank[g][:, 2 * P:], ACT.Copy).then_inc(d["qmat"], 1)
                v("k_turned", 0, 1)
                act.activation(k_tok[:], bank[2][:, 0:KSET * P].rearrange("p (h e) -> p h e", h=KSET), ACT.Copy) \
                    .then_inc(d["k_copied"], 1)
                delta_slot(s, n, 2)
                for g in range(KSET):
                    v("tri0_turned", g, 2)
                    act.activation(tri[:, 2 * g:2 * g + 2, :, :].rearrange("p h c n -> p (h c n)"), bank[2 + g][:],
                                   ACT.Copy).then_inc(d["tri_ready"], 1)
                v("decay_diag", 1, 2)
                v("k_copied", 0, 1)
                for h_ in range(SET):
                    act.activation(k_tail[:, h_, :], k_tok[:, h_ // 2, :], ACT.Copy,
                                   scale=decay[:, h_, 0, P - 1:P]).then_inc(d["k_tail"], 1)
                delta_slot(s, n, 3)
                delta_slot(s, n, 4)

                def scaled(c):
                    for h_ in range(SET):
                        act.activation(v_new[c][:, h_, :], bank[2 + c][:, h_ * P:(h_ + 1) * P], ACT.Copy,
                                       scale=beta_tok[:, c, SET * n + h_:SET * n + h_ + 1]) \
                            .then_inc(d["v0" if c == 0 else "v1"], 1)
                v("r0", 0, 1)
                scaled(0)
                delta_slot(s, n, 5)
                v("s1", 0, 1)
                act.activation(state[:], bank[3][:].rearrange("p (h e) -> p h e", h=SET), ACT.Copy) \
                    .then_inc(d["s1_copied"], 1)
                if n + 1 < SETS:
                    delta_norm_root(n + 1)
                delta_slot(s, n, 6)
                v("r1", 0, 1)
                scaled(1)
                delta_slot(s, n, 7)
                for g in range(2):
                    v("o_sum", g, 2)
                    o = o_all[:, SET * n + 2 * g:SET * n + 2 * g + 2, :]
                    act.activation(o, bank[g][:].rearrange("p (h t) -> p h t", h=2), ACT.Copy) \
                        .then_inc(d["o_copied"], 1)
                    v("o_copied", g, 2)
                    if n or g:
                        act.wait_ge(d["o_sums"], 2 * n + g)
                    act.activation(psq[:, 0, :].rearrange("p (h t) -> p h t", h=2), o, ACT.Square) \
                        .then_inc(d["o_squared"], 1)

            def delta(s):
                hi_to(first_panel[s] + 4)
                delta_gates(s)
                for j in range(8):
                    hi_to(first_panel[s] + 1 + j + 3)
                    delta_tile(s, 0, j)
                    if j == 3:
                        act.wait_ge(d["gate_tok"], 1)
                        act.activation(neg_eg[:], g_tok[:], ACT.Exp).then_inc(d["tok_exp"], 1)
                delta_norm_root(0)
                for n in range(SETS):
                    delta_set(s, n)
                act.wait_ge(d["o_added"], 1)
                act.activation(o_norm[:, 1, :], o_norm[:, 0, :], ACT.Sqrt).then_inc(d["o_root"], 1)

            act.wait_ge(cols_loaded, 16)
            act.wait_ge(consts_ready, 2)
            hi_to(1)
            prepare(0)
            for s in range(n_stages):
                if stages[s][0] == DELTA:
                    delta(s)
                if stages[s][0] == HYBRID:
                    hybrid(s)
                blocks_of(s)
                finish(s)
                if s + 1 < n_stages:
                    prepare(s + 1)

        @block.vector
        def _(dve):
            split = [0]
            links = [0]

            def link(ins):
                links[0] += 1
                ins.then_inc(dve_seq, 1)
                dve.wait_ge(dve_seq, links[0])

            def lo(p, turn=None):
                slot = p % RING
                dve.wait_ge(hi_done, used(p, turn))
                dve.tensor_tensor(wlo[slot][:], raw[slot][:], whi[slot][:].bitcast(F32), ALU.subtract) \
                    .then_inc(lo_done, 1)

            def lo_to(last):
                for p in range(split[0], min(last + 1, n_panels)):
                    lo(p)
                split[0] = max(split[0], last + 1)

            def prepare_tile(s, k):
                wait_x(dve, s, k)
                dve.wait_ge(xhi_ready, s * KT + k + 1)
                dve.scalar_tensor_tensor(out=xlo[:, k, :], in0=x[:, k, :], scalar=col(("pre", s), k),
                                         in1=xhi[:, k, :].bitcast(F32), op0=ALU.mult, op1=ALU.subtract) \
                    .then_inc(xlo_ready, 1)

            def prepare_rstd(s):
                dve.wait_ge(sum_ready, KT * (s + 1))
                dve.tensor_scalar(ms[:], bank[6][:, S:2 * S], 1.0 / D, EPS, ALU.mult, ALU.add).then_inc(ms_ready, 1)
                dve.wait_ge(root_ready, s + 1)
                dve.reciprocal(rstd[:], rt[:]).then_inc(rstd_ready, 1)
                dve.wait_ge(rstd_ready, s + 1)

            def finish(s):
                n = posts_before(s)
                if post_norm(s):
                    half = 4.0 if stages[s][0] == FFN2 else 1.0
                    dve.wait_ge(psq_used, 4 * (n + 1))
                    dve.tensor_scalar(ms[:], bank[6][:, 0:S], half / D, half * EPS, ALU.mult, ALU.add) \
                        .then_inc(post_ms_ready, 1)
                    dve.wait_ge(post_root_ready, n + 1)
                    link(dve.reciprocal(prstd[:], rt[:]))

                def update(k):
                    if not post_norm(s) and k % 2 == 0:
                        wait_acc(dve, s, k // 2)
                    if stages[s][0] == HYBRID:
                        dve.scalar_tensor_tensor(out=x[:, k, :], in0=acc(k), scalar=0.5, in1=x[:, k, :],
                                                 op0=ALU.mult, op1=ALU.add).then_inc(x_updated, 1)
                    elif post_norm(s):
                        link(dve.scalar_tensor_tensor(out=tmp[:, k % 2, :], in0=acc(k), scalar=col(("post", s), k),
                                                      in1=prstd[:], op0=ALU.mult, op1=ALU.mult))
                        dve.tensor_tensor(x[:, k, :], x[:, k, :], tmp[:, k % 2, :], ALU.add).then_inc(x_updated, 1)
                    else:
                        dve.tensor_tensor(x[:, k, :], x[:, k, :], acc(k), ALU.add).then_inc(x_updated, 1)
                more = s + 1 < n_stages
                for k in range(KT + 2):
                    if k < KT:
                        update(k)
                    if more and k >= 2:
                        prepare_tile(s + 1, k - 2)
                if more:
                    prepare_rstd(s + 1)

            def ffn_block(s, f, turn):
                kind, sl = stages[s][0], f % 2
                b = plus(first_block[s] + f, turn, UNROLL)
                c = plus(convs_before(s) + f, turn, UNROLL)
                pair = bank[4 + sl]
                dve.wait_ge(panel_used, used(up_panel(s, f, min(1, n_up(s) - 1)), turn))
                if kind == DELTA:
                    dve.tensor_tensor(first[:, sl, 2:], pair[:, 0:S], rstd[:], ALU.mult).then_inc(gate_scaled, 1)
                    dve.wait_ge(d["o_rows"], f + 1)
                    dve.scalar_tensor_tensor(out=second[:, sl, :], in0=o_all[:, f, :], scalar=col(("out_norm", s)),
                                             in1=bank[6 + sl][:, 0:S], op0=ALU.mult, op1=ALU.mult) \
                        .then_inc(pair_read, 1)
                elif kind == HYBRID:
                    dve.wait_ge(y["merged"], 3 * KT * (hybrids_before(s) + 1))
                    for j, (dst, src) in enumerate(((second, pair[:, 0:S]), (third, pair[:, S:]),
                                                    (conv, bank[6 + sl][:, 0:S]))):
                        last = dve.scalar_tensor_tensor(out=dst[:, sl, :], in0=merge[:, j * KT + f, :], scalar=1.0,
                                                        in1=src, op0=ALU.add, op1=ALU.mult)
                        last.then_inc((gate_scaled, y["gated"], pair_read)[j], 1)
                    dve.wait_ge(y["gated"], KT * hybrids_before(s) + f + 1)
                    dve.wait_ge(gate_scaled, b + 1)
                    link(dve.tensor_tensor(second[:, sl, :], second[:, sl, :], third[:, sl, :], ALU.add))
                    dve.wait_ge(pair_read, b + 1)
                    dve.tensor_tensor(h[:, sl, :], second[:, sl, :], conv[:, sl, :], ALU.add).then_inc(h_done, 1)
                    dve.wait_ge(hhi_done, b + 1)
                    dve.tensor_tensor(hlo[:, sl, :], h[:, sl, :], hhi[:, sl, :].bitcast(F32), ALU.subtract) \
                        .then_inc(hlo_done, 1)
                    return
                elif kind == SHORT:
                    m = products_before(s) + f
                    dve.tensor_tensor(third[:, sl, :], pair[:, 0:S], rstd[:], ALU.mult)
                    dve.tensor_tensor(second[:, sl, :], pair[:, S:], rstd[:], ALU.mult).then_inc(product_done, 1)
                    dve.wait_ge(product_done, m + 1)
                    dve.tensor_tensor(first[:, sl, 2:], third[:, sl, :], second[:, sl, :], ALU.mult) \
                        .then_inc(gate_scaled, 1)
                    dve.wait_ge(gate_scaled, b + 1)
                    dve.wait_ge(panel_used, used(up_panel(s, f, 2)))
                    dve.tensor_tensor(second[:, sl, :], bank[7 - sl][:, 0:S], rstd[:], ALU.mult) \
                        .then_inc(pair_read, 1)
                else:
                    dve.tensor_tensor(first[:, sl, 2:], pair[:, 0:S], rstd[:], ALU.mult).then_inc(gate_scaled, 1)
                    dve.tensor_tensor(second[:, sl, :], pair[:, S:], rstd[:], ALU.mult).then_inc(pair_read, 1)
                dve.wait_ge(gate_scaled, b + 1)
                dve.wait_ge(pair_read, b + 1)
                if kind in (FFN1, SHORT):
                    dve.wait_ge(tap_done, c + 1)
                    dve.scalar_tensor_tensor(out=conv[:, sl, :], in0=first[:, sl, 1:S + 1], scalar=tap(s, 1, f, turn),
                                             in1=conv[:, sl, :], op0=ALU.mult, op1=ALU.add).then_inc(conv_seq, 1)
                    dve.wait_ge(conv_seq, c + 1)
                    dve.scalar_tensor_tensor(out=conv[:, sl, :], in0=first[:, sl, 0:S], scalar=tap(s, 0, f, turn),
                                             in1=conv[:, sl, :], op0=ALU.mult, op1=ALU.add).then_inc(conv_done, 1)
                if kind == SHORT:
                    dve.wait_ge(conv_done, c + 1)
                    gated = conv
                else:
                    a = plus(acts_before(s) + f, turn, UNROLL)
                    dve.wait_ge(act_done, a + 1)
                    gated = act_out
                dve.tensor_tensor(h[:, sl, :], gated[:, sl, :], second[:, sl, :], ALU.mult).then_inc(h_done, 1)
                dve.wait_ge(hhi_done, b + 1)
                dve.tensor_tensor(hlo[:, sl, :], h[:, sl, :], hhi[:, sl, :].bitcast(F32), ALU.subtract) \
                    .then_inc(hlo_done, 1)

            def blocks_of(s):
                def body(f, turn):
                    nb = n_blocks(s)
                    if turn is not None:
                        for j in range(n_up(s) + 1):
                            lo(up_panel(s, f + 1, j), turn)
                        split[0] = up_panel(s, nb - 2, n_up(s)) + 1
                    elif f + 1 < nb:
                        lo_to(up_panel(s, f + 1, n_up(s)))
                    else:
                        lo_to(down_panel(s, f))
                    ffn_block(s, f, turn)
                    if f == nb - 1:
                        lo_to(down_panel(s, f) + lead(s))
                run_blocks(dve, s, body)

            def hybrid(s):
                n = hybrids_before(s)
                v = lambda name, i, per: dve.wait_ge(y[name], per * n + i + 1)
                p0 = first_panel[s]
                n_feat = TILES - len(TOKEN_TILES)

                def start():
                    g = col_at[("qk_gain", s)]
                    dve.tensor_copy(qk_gain[:], cols[:, g:g + 8]).then_inc(y["gains"], 1)
                    v("gains", 0, 2)
                    dve.tensor_scalar(qk_gain[:, 2:6], cols[:, g + 2:g + 6], -(HD ** -0.5), None, ALU.mult) \
                        .then_inc(y["gains"], 1)
                    dve.tensor_scalar(gla_gain[:], col(("gla_gain", s)), 0.5, None, ALU.mult) \
                        .then_inc(y["gla_gained"], 1)

                def tile(t):
                    if t in TOKEN_TILES:
                        return
                    dve.wait_ge(panel_used, used(p0 + t))
                    if n == 0 and t == FIRST_MERGE:
                        dve.wait_ge(y["zeroed"], 3)
                    src, dst = bank[4 + unit(t) % 2], feature_tile(t)
                    rows = dst.shape[0]
                    if t == FIRST_GLA or t == FIRST_GLA + 1:
                        last = dve.scalar_tensor_tensor(out=dst, in0=src[:, 0:S], scalar=HD ** -0.5, in1=rstd[:],
                                                        op0=ALU.mult, op1=ALU.mult)
                    else:
                        last = dve.tensor_tensor(dst, src[0:rows, 0:S], rstd[0:rows, :], ALU.mult)
                    last.then_inc(y["tile_read"], 1)
                    if t == 1:
                        dve.wait_ge(y["small_loaded"], 64 * (n + 1))
                        v("tile_read", 1, n_feat)
                        by = kcv.rearrange("p (c t) -> p t c", t=STEP)
                        for j in range(CMP // STEP):
                            dve.tensor_copy(cmp_x[:, j * STEP:(j + 1) * STEP, 0:NCMP], by[:, :, j:j + NCMP]) \
                                .then_inc(y["cmp_x"], 1)
                        dve.tensor_copy(cmp_x[:, :, NCMP], pos).then_inc(y["cmp_x"], 1)

                def before(t):
                    if t == 3:
                        v("turned", 0, 1)
                        dve.tensor_copy(rstd_tok[:], bank[7][:, 0:2 * P].rearrange("p (c q) -> p c q", c=2)[:, :, 0]) \
                            .then_inc(y["tok_rstd"], 1)
                        if n == 0:
                            dve.wait_ge(y["table_product"], 1)
                            dve.tensor_tensor(table, bank[3][0:2 * HEADS, 0:TABLE], table, ALU.add) \
                                .then_inc(y["table"], 1)

                def step(k):
                    if k == 0:
                        v("low_gate", GATE_STEPS.index("gate_product"), len(GATE_STEPS))
                        for a in range(2):
                            link(dve.tensor_scalar(gsum[:, a, :], bank[3][:, a * S:(a + 1) * S],
                                                   col(("gate_b", s), a), None, ALU.add))
                        dve.scalar_tensor_tensor(out=conv[:, :, :], in0=gsum, scalar=-1.0, in1=gsum,
                                                 op0=ALU.mult, op1=ALU.max).then_inc(y["low_gate"], 1)
                        v("qk_sums", 1, 2)
                        dve.tensor_scalar(qk_ms[:, 0, :], bank[2][:, 0:32], 1.0 / HD, EPS, ALU.mult, ALU.add) \
                            .then_inc(y["qk_ms"], 1)
                        v("cmp_hidden", 0, 1)
                        dve.tensor_copy(cmp_small[:, 0:1], bank[0][:, NCMP:NCMP + 1]).then_inc(y["cmp_bias"], 1)
                        v("low_gate", GATE_STEPS.index("gate_ln"), len(GATE_STEPS))
                        link(dve.scalar_tensor_tensor(out=third[:, :, :], in0=gsum, scalar=0.0, in1=conv[:, :, :],
                                                      op0=ALU.min, op1=ALU.subtract))
                        for a in range(2):
                            dve.tensor_tensor_scan(gsum[:, a, :], ones_row, third[:, a, :], 0.0, ALU.mult, ALU.add) \
                                .then_inc(y["gsum"], 1)
                        v("low_tanh", 0, 1)
                        g = lowrank[ROW_G:ROW_G + 3 * HEADS, :]
                        dve.tensor_scalar(g, g, 0.5, 0.5, ALU.mult, ALU.add).then_inc(y["gsum"], 1)
                        v("qk_root", 0, 1)
                        dve.reciprocal(qk_inv[:], qk_ms[:, 1, :]).then_inc(y["qk_inv"], 1)
                    if k == 1:
                        v("gains", 1, 2)
                        for i in range(8):
                            v("qk_rows", i // 2, 4)
                            last = dve.scalar_tensor_tensor(out=qkn[:, i, :], in0=qkn[:, i, :],
                                                            scalar=qk_gain[:, i:i + 1],
                                                            in1=bank[i // 2][:, (i % 2) * S:(i % 2 + 1) * S],
                                                            op0=ALU.mult, op1=ALU.mult)
                        last.then_inc(y["qk_ready"], 1)
                    if k == 2:
                        v("cmp_kv", 0, 1)
                        dve.tensor_copy(cmp_raw, bank[0][:, 0:NCMP]).then_inc(y["kc_norm"], 1)
                        dve.tensor_copy(cmp_v, bank[1][0:NCMP, 0:HD]).then_inc(y["vc_copied"], 1)
                    if k == 3:
                        v("kc_norm", KC_STEPS.index("kc_sum"), len(KC_STEPS))
                        dve.tensor_scalar(cmp_ms, bank[0][:, 0:NCMP], 0.5 / HD, EPS, ALU.mult, ALU.add) \
                            .then_inc(y["kc_norm"], 1)
                        v("kc_norm", KC_STEPS.index("kc_root"), len(KC_STEPS))
                        link(dve.reciprocal(cmp_ms, cmp_ms))
                        dve.scalar_tensor_tensor(out=cmp_k, in0=cmp_raw, scalar=col(("cmp_gain", s)), in1=cmp_ms,
                                                 op0=ALU.mult, op1=ALU.mult).then_inc(y["kc_norm"], 1)
                    if k == 4:
                        v("cmp_attn", CMP_STEPS.index("cmp_scores"), len(CMP_STEPS))
                        mask = cmp_masks.rearrange("p m (a n) -> p m a n", a=8)
                        for b in range(2):
                            src = bank[b][:, 0:64].rearrange("p (a n) -> p a n", a=4)[:, :, 0:NCMP]
                            last = dve.tensor_tensor(cmp_p[:, 4 * b:4 * b + 4, :], src,
                                                     mask[:, 1, 4 * b:4 * b + 4, :], ALU.add)
                        link(last)
                        link(dve.tensor_reduce(cmp_max, cmp_p, AX.X, ALU.min))
                        dve.tensor_tensor(cmp_p, cmp_p, cmp_max.rearrange("p (a n) -> p a n", n=1)
                                          .to_broadcast([P, 8, NCMP]), ALU.subtract).then_inc(y["cmp_attn"], 1)
                    if k == 5:
                        v("cmp_attn", CMP_STEPS.index("cmp_exp"), len(CMP_STEPS))
                        mask = cmp_masks.rearrange("p m (a n) -> p m a n", a=8)
                        link(dve.tensor_reduce(cmp_sum, cmp_p, AX.X, ALU.add))
                        link(dve.reciprocal(cmp_sum, cmp_sum))
                        link(dve.tensor_tensor(cmp_p, cmp_p, mask[:, 0, :, :], ALU.mult))
                        dve.tensor_tensor(cmp_p, cmp_p, cmp_sum.rearrange("p (a n) -> p a n", n=1)
                                          .to_broadcast([P, 8, NCMP]), ALU.mult).then_inc(y["cmp_attn"], 1)
                    u = k - ATTN_SLOT
                    if 0 <= u < NU:
                        _, _, b, head, _, _ = attn(u)
                        v("s_sum", u, NU)
                        if u == 0:
                            dve.wait_ge(y["rel_loaded"], 16)
                        if u >= 2:
                            v("p_ready", u - 2, NU)
                        for r, (cs, rs) in enumerate(((slice(0, P), slice(P, S)), (slice(P, 3 * P), slice(0, S)))):
                            last = dve.tensor_tensor_reduce(out=logits[:, b, cs], in0=bank[b][:, cs],
                                                            in1=rel[:, head, rs], scale=1.0, scalar=-NEG * 10,
                                                            op0=ALU.add, op1=ALU.min,
                                                            accum_out=row_min[:, b, r:r + 1])
                        last.then_inc(y["t_ready"], 1)
                    li = k - LEVEL_SLOT + 1
                    if 0 <= li < NL - 1:
                        seg = SEGMENTS[li]
                        if li:
                            v("e_ready", li - 1, NL - 1)
                        by = lambda t: t.rearrange("p a (g t) -> p (a g) t", t=seg)
                        dve.tensor_tensor(by(second[:, :, :]), by(gsum), by(gsum)[:, :, seg // 2 - 1:seg // 2]
                                          .to_broadcast([P, 2 * S // seg, seg]), ALU.subtract).then_inc(y["diff"], 1)
                    li = k - LEVEL_SLOT
                    if 0 <= li < NL:
                        w = 2 * (li % 2)
                        v("level_sum", li, NL)
                        if li >= 2:
                            v("a_ready", li - 1, NL)
                        for b in range(2):
                            if li == 0:
                                last = dve.tensor_copy(a_cross[:, b, :, :],
                                                       bank[b][:, 0:2 * P].rearrange("p (a i) -> p a i", a=2))
                            else:
                                last = dve.copy_predicated(
                                    a_diag[b], level_masks[:, li - 1:li, :].to_broadcast([P, 4, P]),
                                    bank[w + b][:].rearrange("p (a i) -> p a i", a=4))
                        last.then_inc(y["a_ready"], 1)
                    li = k - LEVEL_SLOT + 1
                    if 1 <= li < NL - 1:
                        v("e_ready", li, NL - 1)
                        dve.tensor_tensor(level_k[li % 2], gqk[:, 2:4, :], first[:, :, 2:], ALU.mult) \
                            .then_inc(y["qe_ready"], 1)
                    if LEVEL_SLOT + 1 <= k < LEVEL_SLOT + 4:
                        j = k - LEVEL_SLOT - 1
                        v("gate_rows", j, 3)
                        o = (o_cmp, o_slc, o_win)[j]
                        g = bank[6 + j % 2][:].rearrange("p (a t) -> p a t", a=2)
                        if j == 0:
                            v("o_cmp", 0, 1)
                            v("o_copied", NU // 2 - 1, NU // 2)
                        last = dve.tensor_tensor(o, o, g, ALU.mult)
                        last.then_inc(y["nsa_gated"], 1)
                        v("nsa_gated", j, 3)
                        if j:
                            last = dve.tensor_tensor(o_cmp, o_cmp, o, ALU.add)
                            if j == 1:
                                link(last)
                            else:
                                last.then_inc(y["nsa"], 1)
                    if k == LEVEL_SLOT + 5:
                        v("out_th", 3, 4)
                        dve.scalar_tensor_tensor(out=sgate, in0=sq[:, :, :], scalar=1.0, in1=sgate,
                                                 op0=ALU.add, op1=ALU.mult).then_inc(y["sgate"], 1)
                    if k == OUT_SLOT + 1:
                        v("gla_norm", GLA_STEPS.index("gla_sums"), len(GLA_STEPS))
                        dve.tensor_scalar(qk_ms[:, 0, 0:8], bank[0][:, 0:8], 1.0 / P, EPS, ALU.mult, ALU.add) \
                            .then_inc(y["gla_norm"], 1)
                        v("gla_norm", GLA_STEPS.index("gla_root"), len(GLA_STEPS))
                        dve.reciprocal(qk_inv[:, 0:8], qk_ms[:, 1, 0:8]).then_inc(y["gla_norm"], 1)
                    if k == OUT_SLOT + 2:
                        v("gla_gained", 0, 1)
                        v("sgate", 0, 1)
                        for g in range(2):
                            v("gla_rows", g, 2)
                            og = o_gla[:, 2 * g:2 * g + 2, :]
                            link(dve.scalar_tensor_tensor(out=og, in0=og, scalar=gla_gain[:],
                                                          in1=bank[2 + g][:].rearrange("p (a t) -> p a t", a=2),
                                                          op0=ALU.mult, op1=ALU.mult))
                            dve.tensor_tensor(og, og, sgate[:, 2 * g:2 * g + 2, :], ALU.mult) \
                                .then_inc(y["gla_ready"], 1)

                def after(k):
                    u = k - ATTN_SLOT
                    if 0 <= u < NU:
                        b = u % 2
                        v("p_ready", u, NU)
                        link(dve.reciprocal(row_inv[:, b, :], row_sum[:, b, :]))
                        for r, cs in enumerate((slice(0, P), slice(P, 3 * P))):
                            last = dve.tensor_scalar(probs[b][:, cs], probs[b][:, cs], row_inv[:, b, r:r + 1], None,
                                                     ALU.mult)
                        last.then_inc(y["p_scaled"], 1)

                start()
                for t in range(TILES):
                    before(t)
                    if t >= FIRST_GLA:
                        step(t - FIRST_GLA)
                    lo_to(p0 + t + 3)
                    tile(t)
                    if t >= FIRST_GLA:
                        after(t - FIRST_GLA)
                for k in range(KT):
                    v("o_hi", k, KT)
                    dve.tensor_tensor(xlo[:, k, :], mixed(k), xhi[:, k, :].bitcast(F32), ALU.subtract) \
                        .then_inc(y["o_lo"], 1)
                lo_to(p0 + TILES + 3)

            def delta_tile(s, n, j):
                t, sl = 8 * n + j, j % 2
                dve.wait_ge(panel_used, used(first_panel[s] + 1 + t))
                if t == 0:
                    dve.wait_ge(consts_ready, 3)
                dve.tensor_tensor(delta_in[:, sl, WIDTH - 1:], bank[4 + sl][:, 0:S], rstd[:], ALU.mult) \
                    .then_inc(d["tile_read"], 1)
                dve.wait_ge(d["tile_read"], t + 1)
                dve.wait_ge(d["tap"], t + 1)
                for w in range(WIDTH - 2, -1, -1):
                    last = dve.scalar_tensor_tensor(out=conv[:, sl, :], in0=delta_in[:, sl, w:w + S],
                                                    scalar=col(("tap", s), w * 4 * KH + t), in1=conv[:, sl, :],
                                                    op0=ALU.mult, op1=ALU.add)
                    if w:
                        link(last)
                last.then_inc(d["convolved"], 1)

            def delta_slot(s, n, j):
                p = first_panel[s] + 1 + 8 * (n + 1) + j
                lo_to(min(p + 3, first_panel[s] + before_blocks(s) + 4))
                if n + 1 < SETS:
                    delta_tile(s, n + 1, j)

            def delta_gates(s):
                a, b = slice(ROW_A, ROW_A + VH), slice(0, VH)
                dve.wait_ge(panel_used, used(first_panel[s]))
                dve.tensor_tensor(gates[b, 0, :], bank[7][b, 0:S], rstd[b, :], ALU.mult).then_inc(d["gates_scaled"], 1)
                link(dve.tensor_tensor(gates[a, 0, :], bank[7][a, 0:S], rstd[a, :], ALU.mult))
                link(dve.tensor_scalar(gates[a, 0, :], gates[a, 0, :], col(("dt_bias", s))[a, :], None, ALU.add))
                dve.scalar_tensor_tensor(out=gates[a, 1, :], in0=gates[a, 0, :], scalar=-1.0, in1=gates[a, 0, :],
                                         op0=ALU.mult, op1=ALU.max).then_inc(d["gates_scaled"], 1)

            def delta_gates_softplus(s):
                a, b = slice(ROW_A, ROW_A + VH), slice(0, VH)
                dve.wait_ge(d["gate_act"], 1)
                link(dve.tensor_scalar(gates[b, 1, :], gates[b, 1, :], 1.0, None, ALU.add))
                dve.reciprocal(gates[b, 0, :], gates[b, 1, :]).then_inc(d["gates_ready"], 1)
                dve.wait_ge(d["gate_act"], 4)
                e, m, ln = gates[a, 2, :], gates[a, 1, :], gates[a, 3, :]
                link(dve.tensor_scalar(m, e, 1.0 / 3, -0.5, ALU.mult, ALU.add))
                link(dve.tensor_tensor(m, m, e, ALU.mult))
                link(dve.scalar_tensor_tensor(out=m, in0=m, scalar=1.0, in1=e, op0=ALU.add, op1=ALU.mult))
                link(dve.tensor_tensor(m, m, ln, ALU.subtract))
                link(dve.scalar_tensor_tensor(out=m, in0=e, scalar=0.01, in1=m, op0=ALU.is_lt, op1=ALU.mult))
                link(dve.tensor_tensor(ln, ln, m, ALU.add))
                link(dve.scalar_tensor_tensor(out=m, in0=gates[a, 0, :], scalar=0.0, in1=ln,
                                              op0=ALU.max, op1=ALU.add))
                link(dve.tensor_scalar(e, m, a_rate[a, :], -1.0, ALU.mult, ALU.mult))
                for c in range(CHUNKS):
                    cs = slice(c * P, (c + 1) * P)
                    dve.tensor_tensor_scan(gates[a, 1, cs], ones[a, :], gates[a, 2, cs], 0.0, ALU.mult, ALU.add) \
                        .then_inc(d["gates_ready"], 1)

            def delta_gates_turned(s):
                dve.wait_ge(d["gate_turned"], 1)
                by_chunk = lambda b, o: bank[b][:, o:o + CHUNKS * VH].rearrange("p (c h) -> p c h", c=CHUNKS)
                dve.tensor_copy(g_tok[:], by_chunk(7, 256)).then_inc(d["gate_tok"], 1)
                dve.tensor_copy(beta_tok[:], by_chunk(6, 0)).then_inc(d["gate_tok"], 1)
                dve.wait_ge(d["gate_tok"], 2)
                link(dve.tensor_scalar(neg_beta[:], beta_tok[:], -1.0, None, ALU.mult))
                dve.wait_ge(d["tok_exp"], 1)
                link(dve.tensor_scalar(neg_eg[:], neg_eg[:], -1.0, None, ALU.mult))

            def delta_norm_ms(n):
                nk = KSET * CHUNKS
                dve.wait_ge(d["norm_sums"], n + 1)
                dve.tensor_scalar(norm_cols[:, 0, 0:nk], bank[6][:, 0:nk], float(P), P * EPS, ALU.mult, ALU.add) \
                    .then_inc(d["norm_ms"], 1)
                dve.tensor_scalar(norm_cols[:, 0, nk:], bank[6][:, nk:2 * nk], EPS, None, ALU.add) \
                    .then_inc(d["norm_ms"], 1)

            def delta_norm_inv(n):
                dve.wait_ge(d["norm_root"], n + 1)
                dve.reciprocal(inv_norm[:], norm_cols[:, 1, :]).then_inc(d["norm_inv"], 1)

            def delta_set(s, n):
                v = lambda name, i, per: dve.wait_ge(d[name], per * n + i + 1)
                q = qk[n % 2]
                delta_slot(s, n, 0)
                for g in range(2):
                    v("norm_rows", g, 2)
                    qs = q[:, 2 * g:2 * g + 2, :]
                    dve.tensor_tensor(qs, qs, bank[2 + g][:].rearrange("p (h t) -> p h t", h=2), ALU.mult) \
                        .then_inc(d["qk_ready"], 1)
                if n:
                    dve.wait_ge(d["qmat"], 4 * n)
                for g in range(KSET):
                    v("g_rows", g, 2)
                    rows = bank[6 + g][:].rearrange("p (h c i) -> p h c i", h=2, c=2)
                    for hh in range(2):
                        for c in range(CHUNKS):
                            head = SET * n + 2 * g + hh
                            last = dve.scalar_tensor_tensor(
                                out=decay[:, 2 * g + hh, c, :], in0=rows[:, hh, c, :],
                                scalar=g_tok[:, c, head:head + 1], in1=masks[:, 8, :],
                                op0=ALU.subtract, op1=ALU.add)
                    last.then_inc(d["exponent"], 1)
                delta_slot(s, n, 1)
                for g in range(KSET):
                    v("products", g, 2)
                    v("decay", g, 2)
                    for hh in range(2):
                        for c in range(CHUNKS):
                            head = SET * n + 2 * g + hh
                            last = dve.scalar_tensor_tensor(
                                out=amat[:, 2 * g + hh, c, :], in0=bank[g][:, c * P:(c + 1) * P],
                                scalar=neg_beta[:, c, head:head + 1], in1=decay[:, 2 * g + hh, c, :],
                                op0=ALU.mult, op1=ALU.mult)
                    last.then_inc(d["amat"], 1)
                flat = lambda t, g: t[:, 2 * g:2 * g + 2, :, :].rearrange("p h c n -> p (h c) n")
                for g in range(KSET):
                    v("amat", g, 2)
                    if n and g == 0:
                        dve.wait_ge(d["o_sum"], 2 * n)
                    dve.tensor_tensor(flat(tri_t, g), flat(amat, g), masks[:, 7:8, :].to_broadcast([P, 4, P]),
                                      ALU.mult).then_inc(d["tri0"], 1)
                for g in range(KSET):
                    v("tri0", g, 4)
                    dve.tensor_tensor(flat(tri_t, g), flat(tri_t, g),
                                      masks[:, 0:1, :].to_broadcast([P, 4, P]), ALU.add).then_inc(d["tri0"], 1)
                delta_slot(s, n, 2)
                for li, level in enumerate(LEVELS):
                    e = len(LEVELS) * n + li
                    flat = lambda t, g: t[:, 2 * g:2 * g + 2, :, :].rearrange("p h c n -> p (h c) n")
                    sums = lambda b: bank[b][:].rearrange("p (m n) -> p m n", m=4)
                    for g in range(KSET):
                        dve.wait_ge(d["w_sum"], KSET * e + g + 1)
                        dve.tensor_tensor(flat(wmat, g), sums(2 + g),
                                          masks[:, 1 + li:2 + li, :].to_broadcast([P, 4, P]), ALU.mult) \
                            .then_inc(d["w_ready"], 1)
                    if li == 0:
                        delta_slot(s, n, 3)
                    if li == 2:
                        delta_slot(s, n, 4)
                    for g in range(KSET):
                        if li < len(LEVELS) - 1:
                            dve.wait_ge(d["t_sum"], KSET * ((len(LEVELS) - 1) * n + li) + g + 1)
                            dve.tensor_tensor(flat(tri, g), flat(tri, g), sums((6, 0)[g]), ALU.add) \
                                .then_inc(d["t_ready"], 1)
                        dve.wait_ge(d["u_sum"], KSET * e + g + 1)
                        dve.tensor_tensor(flat(tri_t, g), flat(tri_t, g), sums((7, 1)[g]), ALU.add) \
                            .then_inc(d["u_ready"], 1)
                delta_slot(s, n, 5)
                if n + 1 < SETS:
                    delta_norm_ms(n + 1)
                delta_slot(s, n, 6)
                v("ks", 0, 1)
                for h_ in range(SET):
                    head = SET * n + h_
                    last = dve.scalar_tensor_tensor(
                        out=v_tok[1][:, h_, :], in0=bank[2][:, h_ * P:(h_ + 1) * P],
                        scalar=neg_eg[:, 1, head:head + 1], in1=v_tok[1][:, h_, :], op0=ALU.mult, op1=ALU.add)
                last.then_inc(d["v1_in"], 1)
                if n + 1 < SETS:
                    delta_norm_inv(n + 1)
                delta_slot(s, n, 7)
                v("o_sums", 1, 2)
                cs = slice(SET * CHUNKS * n, SET * CHUNKS * (n + 1))
                dve.tensor_scalar(o_norm[:, 0, cs], bank[7][:, 0:SET * CHUNKS], 1.0 / P, EPS, ALU.mult, ALU.add) \
                    .then_inc(d["o_added"] if n == SETS - 1 else d["gate_seq"], 1)

            def delta(s):
                lo_to(first_panel[s] + 4)
                delta_gates(s)
                for j in range(8):
                    lo_to(first_panel[s] + 1 + j + 3)
                    delta_tile(s, 0, j)
                    if j == 0:
                        delta_gates_softplus(s)
                    if j == 3:
                        delta_gates_turned(s)
                delta_norm_ms(0)
                delta_norm_inv(0)
                for n in range(SETS):
                    delta_set(s, n)
                dve.wait_ge(d["o_root"], 1)
                dve.reciprocal(o_inv[:], o_norm[:, 1, :]).then_inc(d["o_inv"], 1)

            dve.wait_ge(cols_loaded, 16)
            dve.wait_ge(masks_loaded, 16)
            dve.wait_ge(consts_ready, 2)
            lo_to(1)
            for k in range(KT):
                prepare_tile(0, k)
            prepare_rstd(0)
            for s in range(n_stages):
                if stages[s][0] == DELTA:
                    delta(s)
                if stages[s][0] == HYBRID:
                    hybrid(s)
                blocks_of(s)
                finish(s)

        @block.tensor
        def _(pe):
            def mm3(dst, w_hi, w_lo, a_hi, a_lo, start, stop):
                pe.matmul(dst, w_hi, a_hi, start=start, stop=False, skip_group_check=True)
                pe.matmul(dst, w_hi, a_lo, start=False, stop=False, skip_group_check=True)
                return pe.matmul(dst, w_lo, a_hi, start=False, stop=stop, skip_group_check=True)

            def up(s, p, turn, dst, prepare=None):
                slot = p % RING
                pe.wait_ge(lo_done, used(p, turn))
                for k in range(KT):
                    if prepare is not None:
                        pe.wait_ge(xlo_ready, prepare * KT + k + 1)
                    last = mm3(dst, whi[slot][:, k * P:(k + 1) * P], wlo[slot][:, k * P:(k + 1) * P],
                               xhi[:, k, :], xlo[:, k, :], k == 0, k == KT - 1)
                    if k == KT - 1:
                        last.then_inc(panel_used, 1)
                    if prepare is not None:
                        n = prepare * KT + k
                        pe.wait_ge(sq_ready, n + 1)
                        pe.matmul(bank[6][:, S:2 * S], ones[:], sq[:, n % 4, :], start=(k == 0), stop=(k == KT - 1),
                                  skip_group_check=True).then_inc(sum_ready, 1)

            def down(s, f, p, turn):
                slot, sl = p % RING, f % 2
                pe.wait_ge(lo_done, used(p, turn))
                pe.wait_ge(hlo_done, plus(first_block[s] + f + 1, turn, UNROLL))
                for m in range(KT):
                    cs = slice(m * P, (m + 1) * P)
                    last = mm3(acc(m), whi[slot][:, cs], wlo[slot][:, cs], hhi[:, sl, :], hlo[:, sl, :],
                               f == 0 and m % 2 == 0, f == n_blocks(s) - 1 and turn is None)
                    if m in (1, 3, 5) and f == n_blocks(s) - 1 and turn is None:
                        last.then_inc(acc_ready, 1)
                last.then_inc(panel_used, 1)

            def blocks_of(s):
                kind = stages[s][0]
                if kind == DELTA:
                    pe.wait_ge(d["o_inv"], 1)

                def body(f, turn):
                    if f >= 2:
                        pe.wait_ge(pair_read, plus(first_block[s] + f - 1, turn, UNROLL))
                    if kind == HYBRID:
                        branches(s, f)
                    for j in range(n_up(s) if kind != HYBRID else 0):
                        dst = bank[7 - f % 2][:, 0:S] if j == 2 else bank[4 + f % 2][:, j * S:(j + 1) * S]
                        if j == 2 and f == 1:
                            pe.wait_ge(ms_ready, s + 1)
                        if kind == DELTA and f < 2:
                            continue
                        up(s, up_panel(s, f, j), turn, dst, s if f == 0 and j == 0 and kind != DELTA else None)
                    if kind == DELTA:
                        for c in range(CHUNKS):
                            i = CHUNKS * f + c
                            last = pe.matmul(bank[6 + f % 2][:, c * P:(c + 1) * P],
                                             o_inv[:, i:i + 1].to_broadcast([P, P]), ident, start=True, stop=True)
                        last.then_inc(d["o_rows"], 1)
                    if f:
                        down(s, f - 1, up_panel(s, f, n_up(s)), turn)
                run_blocks(pe, s, body)
                down(s, n_blocks(s) - 1, down_panel(s, n_blocks(s) - 1), None)

            def finish(s):
                if not post_norm(s):
                    return
                n = posts_before(s)
                for q in range(KT // 2):
                    pe.wait_ge(psq_ready, 4 * n + q + 1)
                    for r in range(2):
                        last = pe.matmul(bank[6][:, 0:S], ones[:], psq[:, q % 2, r * S:(r + 1) * S],
                                         start=(q + r == 0), stop=(q == KT // 2 - 1 and r == 1),
                                         skip_group_check=True)
                        if r:
                            last.then_inc(psq_used, 1)

            def hybrid(s):
                n = hybrids_before(s)
                v = lambda name, i, per: pe.wait_ge(y[name], per * n + i + 1)
                p0 = first_panel[s]
                n_feat = TILES - len(TOKEN_TILES)

                def tile(t):
                    dst = bank[4 + unit(t) % 2]
                    second_half = t - 1 in VALUE_PAIRS
                    if unit(t) >= 2 and not second_half:
                        w = max(w for w in range(t) if unit(w) == unit(t) - 2)
                        if w in TOKEN_TILES:
                            v("tok_read", tok_units(w), N_TOK)
                        else:
                            v("tile_read", w - tok_tiles(w), n_feat)
                    p = p0 + t
                    if t not in TOKEN_TILES:
                        up(s, p, None, dst[:, 0:S], s if t == 0 else None)
                        return
                    slot = p % RING
                    pe.wait_ge(lo_done, used(p))
                    paired = second_half or t in VALUE_PAIRS
                    w, nk = (S, KT // 2) if paired else (P, KT)
                    k0 = nk if second_half else 0
                    for c in range(CHUNKS):
                        for k in range(nk):
                            last = mm3(dst[:, c * w:(c + 1) * w], xhi[:, k0 + k, chunk(c)], xlo[:, k0 + k, chunk(c)],
                                       whi[slot][:, k * w:(k + 1) * w], wlo[slot][:, k * w:(k + 1) * w],
                                       k0 + k + c == 0, k0 + k == KT - 1)
                    last.then_inc(panel_used, 1)

                def square_sums(part):
                    v("squared", 4 * part + 3, 8)
                    for i in range(4 * part, 4 * part + 4):
                        for c in range(CHUNKS):
                            o = 2 * (CHUNKS * i + c)
                            last = pe.matmul(bank[2][:, o:o + 2], sq[:, i % 4, chunk(c)], halves[:], start=True, stop=True)
                    last.then_inc(y["qk_sums"], 1)

                def before(t):
                    if t == 3:
                        pe.wait_ge(rstd_ready, s + 1)
                        for c in range(CHUNKS):
                            last = pe.transpose(bank[7][:, chunk(c)], rstd[:, chunk(c)], ident)
                        last.then_inc(y["turned"], 1)
                        if n == 0:
                            pe.wait_ge(y["consts"], 16 * 6)
                            pe.matmul(bank[3][0:2 * HEADS, 0:TABLE], rel_table[:], onehot, start=True, stop=True) \
                                .then_inc(y["table_product"], 1)
                    if t == 9:
                        square_sums(0)

                def step(k):
                    if k == 0:
                        pe.wait_ge(y["small_loaded"], 64 * (n + 1))
                        if n == 0:
                            pe.wait_ge(y["table"], 1)
                        for a in range(2):
                            last = pe.matmul(bank[3][:, a * S:(a + 1) * S], gate_w[:, chunk(a)], lowrank[0:RANK, :],
                                             start=True, stop=True)
                        last.then_inc(y["low_gate"], 1)
                        square_sums(1)
                        v("cmp_x", 2, 3)
                        for q in range(CMP):
                            last = pe.matmul(bank[0][:, 0:NCMP + 1], w1[:, q, :], cmp_x[:, q, :],
                                             start=(q == 0), stop=(q == CMP - 1))
                        last.then_inc(y["cmp_hidden"], 1)
                    if k == 1:
                        v("qk_inv", 0, 1)
                        v("cmp_act", 0, 1)
                        v("gsum", 0, 3)
                        for i in range(8):
                            for c in range(CHUNKS):
                                o = 2 * (CHUNKS * i + c)
                                for b in range(2):
                                    last = pe.matmul(
                                        bank[i // 2][half(b), (i % 2) * S + c * P:(i % 2) * S + (c + 1) * P],
                                        qk_inv[:, o + b:o + b + 1].to_broadcast([P, HD]), ident, start=True, stop=True)
                            if i % 2:
                                last.then_inc(y["qk_rows"], 1)
                    if k == 2:
                        v("qk_ready", 0, 1)
                        pe.matmul(bank[0][:, 0:NCMP], w2[0:HD, :], cmp_hid[0:HD, :], start=True, stop=True)
                        pe.matmul(bank[1][0:NCMP, 0:HD], cmp_hid[HD:, :], w2[HD:, 0:HD], start=True, stop=True) \
                            .then_inc(y["cmp_kv"], 1)
                    if k == 3:
                        v("kc_norm", KC_STEPS.index("kc_squared"), len(KC_STEPS))
                        pe.matmul(bank[0][:, 0:NCMP], ones[:], cmp_sq, start=True, stop=True).then_inc(y["kc_norm"], 1)
                    if k == 4:
                        v("kc_norm", KC_STEPS.index("kc_ready"), len(KC_STEPS))
                        v("vc_copied", 0, 1)
                        for b in range(2):
                            for a in range(2):
                                for c in range(CHUNKS):
                                    o = 16 * (2 * a + c)
                                    last = pe.matmul(bank[b][:, o:o + NCMP], qkn[half(b), 2 + a, chunk(c)],
                                                     cmp_k[half(b), :], start=True, stop=True)
                        last.then_inc(y["cmp_attn"], 1)
                    if k == 6:
                        v("cmp_attn", CMP_STEPS.index("cmp_p"), len(CMP_STEPS))
                        for i in range(8):
                            last = pe.transpose(bank[2 + i // 4][0:NCMP, chunk(i % 4)], cmp_p[:, i, :], ident)
                        last.then_inc(y["cmp_attn"], 1)
                    if k == 7:
                        v("cmp_attn", CMP_STEPS.index("cmp_pt2"), len(CMP_STEPS))
                        for b in range(2):
                            for i in range(4):
                                last = pe.matmul(bank[6][half(b), chunk(i)], cmp_v, cmp_t[b][:, chunk(i)],
                                                 start=True, stop=True)
                        last.then_inc(y["cmp_attn"], 1)
                    u = k - ATTN_SLOT
                    if 0 <= u < NU:
                        qt, kt, b, _, _, _ = attn(u)
                        if u >= 2:
                            v("t_ready", u - 2, NU)
                        pe.matmul(bank[b][:, 0:P], qkn[half(b), qt, 0:P], qkn[half(b), kt, 0:P], start=True, stop=True)
                        pe.matmul(bank[b][:, P:3 * P], qkn[half(b), qt, P:], qkn[half(b), kt, :], start=True,
                                  stop=True).then_inc(y["s_sum"], 1)
                    if 0 <= u - 1 < NU:
                        w = u - 1
                        v("p_scaled", w, NU)
                        if w >= 2:
                            v("pt_ready", w - 2, NU)
                        for i in range(3):
                            last = pe.transpose(bank[2 + w % 2][:, chunk(i)], probs[w % 2][:, chunk(i)], ident)
                        last.then_inc(y["p_turned"], 1)
                    if 0 <= u - 2 < NU:
                        w = u - 2
                        _, _, b, _, val, _ = attn(w)
                        g = w // 2
                        v("pt_ready", w, NU)
                        if g >= 2:
                            v("o_copied", g - 2, NU // 2)
                        elif g == 0 and b == 0:
                            v("o_cmp", 0, 1)
                        dst, pt = bank[6 + g % 2][half(b), :], probs_t[w % 2]
                        pe.matmul(dst[:, 0:P], val[:, 0, :], pt[:, 0:P], start=True, stop=True)
                        pe.matmul(dst[:, P:S], val[:, 0, :], pt[:, P:2 * P], start=True, stop=False)
                        pe.matmul(dst[:, P:S], val[:, 1, :], pt[:, 2 * P:3 * P], start=False, stop=True) \
                            .then_inc(y["o_sum"], 1)
                    li = k - LEVEL_SLOT
                    if 0 <= li < NL:
                        w = 2 * (li % 2)
                        if li < NL - 1:
                            pe.wait_ge(y["qe_ready"], 2 * ((NL - 1) * n + li + 1))
                            lq, lk = level_q[li % 2], level_k[li % 2]
                        else:
                            lq, lk = gqk[:, 0:2, :], gqk[:, 2:4, :]
                        if li >= 2:
                            v("a_ready", li - 2, NL)
                        for b in range(2):
                            for a in range(2):
                                if li == 0:
                                    last = pe.matmul(bank[b][:, chunk(a)], lk[half(b), a, 0:P], lq[half(b), a, P:S],
                                                     start=True, stop=True)
                                    continue
                                for c in range(CHUNKS):
                                    last = pe.matmul(bank[w + b][:, chunk(2 * a + c)], lk[half(b), a, chunk(c)],
                                                     lq[half(b), a, chunk(c)], start=True, stop=True)
                        last.then_inc(y["level_sum"], 1)
                    if LEVEL_SLOT + 1 <= k < LEVEL_SLOT + 4:
                        j = k - LEVEL_SLOT - 1
                        v("gsum", 2, 3)
                        if j == 2:
                            v("nsa_gated", 0, 3)
                        elif j == 0:
                            v("o_copied", NU // 2 - 2, NU // 2)
                        else:
                            v("o_copied", NU // 2 - 1, NU // 2)
                        for a in range(2):
                            for b in range(2):
                                r = ROW_G + (2 * a + b) * 3 + j
                                last = pe.matmul(bank[6 + j % 2][half(b), a * S:(a + 1) * S],
                                                 ident[ROW_G:ROW_G + 3 * HEADS, r:r + 1]
                                                 .to_broadcast([3 * HEADS, HD]),
                                                 lowrank[ROW_G:ROW_G + 3 * HEADS, :], start=True, stop=True)
                        last.then_inc(y["gate_rows"], 1)
                    if k == OUT_SLOT:
                        v("a_ready", NL - 1, NL)
                        v("nsa", 0, 1)
                        for g in range(2):
                            for hh in range(2):
                                head = 2 * g + hh
                                a, b = g, hh
                                o, val = hh * S, slice(head * P, (head + 1) * P)
                                pe.matmul(bank[6 + g][:, o:o + P], gv[:, 0, val], a_diag[b][:, 2 * a, :],
                                          start=True, stop=True)
                                pe.matmul(bank[6 + g][:, o + P:o + S], gv[:, 0, val], a_cross[:, b, a, :],
                                          start=True, stop=False)
                                last = pe.matmul(bank[6 + g][:, o + P:o + S], gv[:, 1, val],
                                                 a_diag[b][:, 2 * a + 1, :], start=False, stop=True)
                            last.then_inc(y["gla_sum"], 1)
                    if k == OUT_SLOT + 1:
                        v("gla_squared", 1, 2)
                        for i in range(8):
                            last = pe.matmul(bank[0][:, i:i + 1], sq[:, i // 2, chunk(i % 2)], ones[:, 0:1],
                                             start=True, stop=True)
                        last.then_inc(y["gla_norm"], 1)
                    if k == OUT_SLOT + 2:
                        v("gla_norm", GLA_STEPS.index("gla_inv"), len(GLA_STEPS))
                        for i in range(8):
                            last = pe.matmul(bank[2 + i // 4][:, chunk(i % 4)], qk_inv[:, i:i + 1].to_broadcast([P, P]),
                                             ident, start=True, stop=True)
                            if i % 4 == 3:
                                last.then_inc(y["gla_rows"], 1)

                for t in range(TILES):
                    before(t)
                    if t >= FIRST_GLA:
                        step(t - FIRST_GLA)
                    tile(t)

            def branches(s, f):
                p, n = up_panel(s, f, 0), hybrids_before(s)
                slot = p % RING
                pe.wait_ge(lo_done, used(p))
                if f < 2:
                    pe.wait_ge(y["tile_read"], (TILES - len(TOKEN_TILES)) * (n + 1) - 1 + f)
                for dst, tiles in ((bank[4 + f % 2][:, 0:S], (0, 1)), (bank[4 + f % 2][:, S:], (2, 3)),
                                   (bank[6 + f % 2][:, 0:S], (4, 5, 6, 7))):
                    for k in tiles:
                        if f == 0:
                            pe.wait_ge(y["o_lo"], KT * n + k + 1)
                        last = mm3(dst, whi[slot][:, k * P:(k + 1) * P], wlo[slot][:, k * P:(k + 1) * P],
                                   xhi[:, k, :], xlo[:, k, :], k == tiles[0], k == tiles[-1])
                last.then_inc(panel_used, 1)

            def delta_tile(s, n, j):
                t = 8 * n + j
                if t >= 2:
                    pe.wait_ge(d["tile_read"], t - 1)
                up(s, first_panel[s] + 1 + t, None, bank[4 + j % 2][:, 0:S])

            def delta_slot(s, n, j):
                if n + 1 < SETS:
                    delta_tile(s, n + 1, j)
                elif j in (5, 6):
                    up(s, up_panel(s, j - 5, 0), None, bank[4 + (j - 5)][:, 0:S])

            def delta_gates(s):
                up(s, first_panel[s], None, bank[7][:, 0:S], s)

            def delta_turn_gates(s):
                pe.wait_ge(d["gates_ready"], 3)
                for c in range(CHUNKS):
                    cs = slice(c * P, (c + 1) * P)
                    o = 256 + VH * c
                    pe.transpose(bank[6][:, VH * c:VH * (c + 1)], gates[0:VH, 0, cs], ident[0:VH, 0:VH])
                    last = pe.transpose(bank[7][:, o:o + VH], gates[ROW_A:ROW_A + VH, 1, cs],
                                        ident[ROW_A:ROW_A + VH, ROW_A:ROW_A + VH])
                last.then_inc(d["gate_turned"], 1)

            def delta_norm_sums(n):
                pe.wait_ge(d["squared"], 2 * KSET * (n + 1))
                if n == 0:
                    pe.wait_ge(d["gate_tok"], 2)
                for j in range(2 * KSET):
                    for c in range(CHUNKS):
                        i = CHUNKS * j + c
                        last = pe.matmul(bank[6][:, i:i + 1], qk_sq[:, j, c * P:(c + 1) * P], ones[:, 0:1],
                                         start=True, stop=True)
                last.then_inc(d["norm_sums"], 1)

            def delta_set(s, n):
                v = lambda name, i, per: pe.wait_ge(d[name], per * n + i + 1)
                q = qk[n % 2]
                nl = len(LEVELS)

                def each(out_bank, lhs, rhs, done):
                    for m in range(4):
                        last = pe.matmul(bank[out_bank][:, m * P:(m + 1) * P], lhs(m), rhs(m), start=True, stop=True)
                    last.then_inc(d[done], 1)

                pe.wait_ge(d["activated"], 8 * (n + 1))
                if n:
                    pe.wait_ge(d["o_copied"], 2 * n)
                for c in range(CHUNKS):
                    for h_ in range(SET):
                        last = pe.transpose(bank[c][:, h_ * P:(h_ + 1) * P], v_feat[:, h_, c * P:(c + 1) * P], ident)
                    last.then_inc(d["v_turned"], 1)
                delta_slot(s, n, 0)
                v("norm_inv", 0, 1)
                for j in range(2 * KSET):
                    for c in range(CHUNKS):
                        i = CHUNKS * j + c
                        last = pe.matmul(bank[2 + j // 2][:, (i % 4) * P:(i % 4 + 1) * P],
                                         inv_norm[:, i:i + 1].to_broadcast([P, P]), ident, start=True, stop=True)
                    if j % 2:
                        last.then_inc(d["norm_rows"], 1)
                if n == 0:
                    pe.wait_ge(d["gate_tok"], 1)
                else:
                    pe.wait_ge(d["gate_seq"], n)
                for h_ in range(SET):
                    r = ROW_A + SET * n + h_
                    last = pe.matmul(bank[6 + h_ // 2][:, (h_ % 2) * S:(h_ % 2 + 1) * S],
                                     ident[ROW_A:ROW_A + VH, r:r + 1].to_broadcast([VH, P]),
                                     gates[ROW_A:ROW_A + VH, 1, :], start=True, stop=True)
                    if h_ % 2:
                        last.then_inc(d["g_rows"], 1)
                delta_slot(s, n, 1)
                v("qk_ready", 1, 2)
                v("v_copied", 1, 2)
                for g in range(KSET):
                    for a, b in ((KSET + g, 0), (g, 2)):
                        for c in range(CHUNKS):
                            cs = slice(c * P, (c + 1) * P)
                            last = pe.matmul(bank[g][:, (b + c) * P:(b + c + 1) * P], q[:, KSET + g, cs], q[:, a, cs],
                                             start=True, stop=True)
                    last.then_inc(d["products"], 1)
                for g in range(KSET):
                    last = pe.transpose(bank[2][:, g * P:(g + 1) * P], q[:, KSET + g, 0:P], ident)
                last.then_inc(d["k_turned"], 1)
                delta_slot(s, n, 2)
                v("k_copied", 0, 1)
                at = lambda t, g: lambda m: t[:, 2 * g + m // 2, m % 2, :]
                for g in range(KSET):
                    v("tri0", 2 + g, 4)
                    for m in range(4):
                        last = pe.transpose(bank[2 + g][:, m * P:(m + 1) * P], at(tri_t, g)(m), ident)
                    last.then_inc(d["tri0_turned"], 1)
                for li in range(nl):
                    for g in range(KSET):
                        if li == 0:
                            v("tri_ready", g, 2)
                        else:
                            pe.wait_ge(d["t_ready"], KSET * ((nl - 1) * n + li - 1) + g + 1)
                            pe.wait_ge(d["w_ready"], KSET * (nl * n + li - 1) + g + 1)
                        each(2 + g, at(amat, g), at(tri, g), "w_sum")
                    if li == 0:
                        delta_slot(s, n, 3)
                    if li == 2:
                        delta_slot(s, n, 4)
                    for g in range(KSET):
                        pe.wait_ge(d["w_ready"], KSET * (nl * n + li) + g + 1)
                        if li == 0:
                            v("exponent", 1, 2)
                            v("eg", 1, 2)
                            v("qmat", 1, 4)
                        else:
                            pe.wait_ge(d["u_ready"], KSET * (nl * n + li - 1) + g + 1)
                        if li < nl - 1:
                            each((6, 0)[g], at(tri_t, g), at(wmat, g), "t_sum")
                        each((7, 1)[g], at(wmat, g), at(tri_t, g), "u_sum")
                pe.wait_ge(d["u_ready"], KSET * nl * (n + 1))
                each(2, lambda m: tri_t[:, m, 0, :], lambda m: v_tok[0][:, m, :], "r0")
                if n + 1 < SETS:
                    delta_norm_sums(n + 1)
                delta_slot(s, n, 5)
                v("v0", SET - 1, SET)
                v("k_tail", SET - 1, SET)
                each(3, lambda m: k_tail[:, m, :], lambda m: v_new[0][:, m, :], "s1")
                v("s1_copied", 0, 1)
                for g in range(KSET):
                    last = pe.matmul(bank[2][:, 2 * g * P:(2 * g + 2) * P], q[:, KSET + g, P:],
                                     state[:, 2 * g:2 * g + 2, :].rearrange("p h e -> p (h e)"), start=True, stop=True)
                last.then_inc(d["ks"], 1)
                delta_slot(s, n, 6)
                v("v1_in", 0, 1)
                each(3, lambda m: tri_t[:, m, 1, :], lambda m: v_tok[1][:, m, :], "r1")
                delta_slot(s, n, 7)
                v("v1", SET - 1, SET)
                v("qmat", 3, 4)
                v("qg", 0, 1)
                for h_ in range(SET):
                    o = (h_ % 2) * S
                    dst = bank[h_ // 2]
                    pe.matmul(dst[:, o:o + P], v_new[0][:, h_, :], qmat[:, h_, 0, :], start=True, stop=True)
                    pe.matmul(dst[:, o + P:o + S], state[:, h_, :], eg_row[:, h_, :], start=True, stop=False)
                    last = pe.matmul(dst[:, o + P:o + S], v_new[1][:, h_, :], qmat[:, h_, 1, :], start=False, stop=True)
                    if h_ % 2:
                        last.then_inc(d["o_sum"], 1)
                for g in range(2):
                    v("o_squared", g, 2)
                    for hh in range(2):
                        for c in range(CHUNKS):
                            i = CHUNKS * (2 * g + hh) + c
                            o = hh * S + c * P
                            last = pe.matmul(bank[7][:, i:i + 1], psq[:, 0, o:o + P], ones[:, 0:1],
                                             start=True, stop=True)
                    last.then_inc(d["o_sums"], 1)

            def delta(s):
                delta_gates(s)
                for j in range(8):
                    delta_tile(s, 0, j)
                    if j == 3:
                        delta_turn_gates(s)
                delta_norm_sums(0)
                for n in range(SETS):
                    delta_set(s, n)

            pe.wait_ge(consts_ready, 2)
            pe.wait_ge(masks_loaded, 16)
            for s in range(n_stages):
                if stages[s][0] == DELTA:
                    delta(s)
                if stages[s][0] == HYBRID:
                    hybrid(s)
                blocks_of(s)
                finish(s)


def kernel(**inputs):
    import numpy as np
    import concourse.bacc as bacc
    from concourse.bass_utils import run_bass_kernel_spmd

    nc = bacc.Bacc("TRN2", target_bir_lowering=False, num_devices=1)
    stages = stage_list()
    arrays = {k: np.ascontiguousarray(v) for k, v in lay_out(stages, inputs).items()}
    args = {k: nc.dram_tensor(k, v.shape, mybir.dt.from_np(v.dtype), kind="ExternalInput").ap()
            for k, v in arrays.items()}
    args["out"] = nc.dram_tensor("out", (P, KT, S), F32, kind="ExternalOutput").ap()
    build(nc, stages, args)
    r = run_bass_kernel_spmd(nc, [arrays], core_ids=[0])
    return r.results[0]["out"].transpose(2, 1, 0).reshape(1, S, D)
```
